# Optimizing a Trainium2 kernel written in Bass

```python
import math
import jax, jax.numpy as jnp
from jax import lax
import numpy as np

D_MODEL = 2048
BATCH = 1
SEQ = 256
DEPTH = 1

MEM_LEN = 256
EPS = 1e-6
ROPE_THETA = 10000.0
MLA_HEADS = 8
MLA_Q_RANK = 512
MLA_KV_RANK = 256
MLA_NOPE = 128
MLA_ROPE = 64
MLA_V = 128
ATTN_Q_BLOCK = 128
MOBA_HEADS = 8
MOBA_HEAD_DIM = 128
MOBA_BLOCK = 256
MOBA_TOPK = 3
MOBA_Q_CHUNK = 16
CROSS_HEADS = 4
CROSS_HEAD_DIM = D_MODEL // CROSS_HEADS
PEER_HEADS = 8
PEER_NKEYS = 128
PEER_N_EXPERTS = PEER_NKEYS * PEER_NKEYS
PEER_DKEY = 256
PEER_TOPK = 16
PEER_TOKEN_CHUNK = 128

MLA_OUT = MLA_HEADS * MLA_V
MOBA_WIDTH = MOBA_HEADS * MOBA_HEAD_DIM
MIX_WIDTH = MLA_OUT + MOBA_WIDTH
IN_COLS = MLA_Q_RANK + MLA_KV_RANK + MLA_ROPE + 3 * MOBA_WIDTH
IN_SPLITS = (MLA_Q_RANK,
             MLA_Q_RANK + MLA_KV_RANK,
             MLA_Q_RANK + MLA_KV_RANK + MLA_ROPE,
             MLA_Q_RANK + MLA_KV_RANK + MLA_ROPE + MOBA_WIDTH,
             MLA_Q_RANK + MLA_KV_RANK + MLA_ROPE + 2 * MOBA_WIDTH)

kernel_name = 'hybrid_mla_moba_peer_layer'

def rms_norm(x, g):
    xf = x.astype(jnp.float32)
    y = xf * lax.rsqrt(jnp.mean(xf * xf, axis=-1, keepdims=True) + EPS)
    return (y * g.astype(jnp.float32)).astype(x.dtype)

def rope(x, positions):
    dim = x.shape[-1]
    half = dim // 2
    inv_freq = jnp.exp(jnp.arange(half, dtype=jnp.float32) * (-2.0 * math.log(ROPE_THETA) / dim))
    ang = positions.astype(jnp.float32)[:, :, None] * inv_freq
    cos = jnp.cos(ang)[:, :, None, :]
    sin = jnp.sin(ang)[:, :, None, :]
    xf = x.astype(jnp.float32)
    x1, x2 = xf[..., :half], xf[..., half:]
    return jnp.concatenate([x1 * cos - x2 * sin, x2 * cos + x1 * sin], axis=-1).astype(x.dtype)

def causal_block_attention(q, k, v, scale):
    B, H, S, _ = q.shape
    dv = v.shape[-1]
    kpos = jnp.arange(S)

    def one(i):
        start = i * ATTN_Q_BLOCK
        qs = lax.dynamic_slice_in_dim(q, start, ATTN_Q_BLOCK, axis=2)
        s = jnp.einsum('bhqd,bhkd->bhqk', qs, k).astype(jnp.float32) * scale
        qpos = start + jnp.arange(ATTN_Q_BLOCK)
        s = jnp.where(kpos[None, :] <= qpos[:, None], s, -jnp.inf)
        p = jax.nn.softmax(s, axis=-1).astype(v.dtype)
        return jnp.einsum('bhqk,bhkd->bhqd', p, v)

    o = lax.map(one, jnp.arange(S // ATTN_Q_BLOCK))
    return o.transpose(1, 0, 3, 2, 4).reshape(B, S, H * dv)

def moba_attention(q, k, v):
    B, H, S, Dh = q.shape
    nb = -(-S // MOBA_BLOCK)
    pad = nb * MOBA_BLOCK - S
    k_pad = jnp.pad(k, ((0, 0), (0, 0), (0, pad), (0, 0)))
    v_pad = jnp.pad(v, ((0, 0), (0, 0), (0, pad), (0, 0)))
    kb = k_pad.reshape(B, H, nb, MOBA_BLOCK, Dh)
    vb = v_pad.reshape(B, H, nb, MOBA_BLOCK, Dh)
    k_eff = min(MOBA_TOPK, nb - 1)
    scale = Dh ** -0.5
    own_blk = jnp.arange(S) // MOBA_BLOCK
    if k_eff > 0:
        kbar = jnp.mean(kb.astype(jnp.float32), axis=3)
        gate = jnp.einsum('bhsd,bhnd->bhsn', q.astype(jnp.float32), kbar)
        past = jnp.arange(nb)[None, :] < own_blk[:, None]
        gate = jnp.where(past, gate, -jnp.inf)
        _, sel_idx = lax.top_k(gate, k_eff)
        sel_valid = sel_idx < own_blk[:, None]
    bi = jnp.arange(B)[:, None, None, None]
    hi = jnp.arange(H)[None, :, None, None]

    def one(ci):
        start = ci * MOBA_Q_CHUNK
        qc = lax.dynamic_slice_in_dim(q, start, MOBA_Q_CHUNK, axis=2)
        qpos = start + jnp.arange(MOBA_Q_CHUNK)
        ob = start // MOBA_BLOCK
        k_own = lax.dynamic_slice_in_dim(k_pad, ob * MOBA_BLOCK, MOBA_BLOCK, axis=2)
        v_own = lax.dynamic_slice_in_dim(v_pad, ob * MOBA_BLOCK, MOBA_BLOCK, axis=2)
        kpos = ob * MOBA_BLOCK + jnp.arange(MOBA_BLOCK)
        s_own = jnp.einsum('bhqd,bhkd->bhqk', qc, k_own).astype(jnp.float32) * scale
        s_own = jnp.where(kpos[None, :] <= qpos[:, None], s_own, -jnp.inf)
        if k_eff == 0:
            p = jax.nn.softmax(s_own, axis=-1).astype(v.dtype)
            return jnp.einsum('bhqk,bhkd->bhqd', p, v_own)
        idx = lax.dynamic_slice_in_dim(sel_idx, start, MOBA_Q_CHUNK, axis=2)
        ok = lax.dynamic_slice_in_dim(sel_valid, start, MOBA_Q_CHUNK, axis=2)
        k_sel = kb[bi, hi, idx]
        v_sel = vb[bi, hi, idx]
        s_sel = jnp.einsum('bhqd,bhqjkd->bhqjk', qc, k_sel).astype(jnp.float32) * scale
        s_sel = jnp.where(ok[..., None], s_sel, -jnp.inf).reshape(B, H, MOBA_Q_CHUNK, k_eff * MOBA_BLOCK)
        p = jax.nn.softmax(jnp.concatenate([s_sel, s_own], axis=-1), axis=-1).astype(v.dtype)
        p_sel = p[..., :k_eff * MOBA_BLOCK].reshape(B, H, MOBA_Q_CHUNK, k_eff, MOBA_BLOCK)
        p_own = p[..., k_eff * MOBA_BLOCK:]
        return (jnp.einsum('bhqjk,bhqjkd->bhqd', p_sel, v_sel)
                + jnp.einsum('bhqk,bhkd->bhqd', p_own, v_own))

    o = lax.map(one, jnp.arange(S // MOBA_Q_CHUNK))
    return o.transpose(1, 0, 3, 2, 4).reshape(B, S, H * Dh)

def memory_cross_attention(hn, mn, w_cq, w_ck, w_cv, w_co):
    B, S, D = hn.shape
    M = mn.shape[1]
    q = (hn @ w_cq).reshape(B, S, CROSS_HEADS, CROSS_HEAD_DIM)
    k = (mn @ w_ck).reshape(B, M, CROSS_HEADS, CROSS_HEAD_DIM)
    v = (mn @ w_cv).reshape(B, M, CROSS_HEADS, CROSS_HEAD_DIM)
    s = jnp.einsum('bshd,bmhd->bhsm', q, k).astype(jnp.float32) * (CROSS_HEAD_DIM ** -0.5)
    p = jax.nn.softmax(s, axis=-1).astype(v.dtype)
    o = jnp.einsum('bhsm,bmhd->bshd', p, v).reshape(B, S, D)
    return o @ w_co

def peer(xn, w_pq, sub_keys1, sub_keys2, expert_u, expert_v):
    B, S, D = xn.shape
    T = B * S
    xt = xn.reshape(T, D)
    q = (xt @ w_pq).reshape(T, PEER_HEADS, 2, PEER_DKEY // 2)
    s1 = jnp.einsum('thd,nd->thn', q[:, :, 0], sub_keys1).astype(jnp.float32)
    s2 = jnp.einsum('thd,nd->thn', q[:, :, 1], sub_keys2).astype(jnp.float32)
    v1, i1 = lax.top_k(s1, PEER_TOPK)
    v2, i2 = lax.top_k(s2, PEER_TOPK)
    cand = (v1[..., :, None] + v2[..., None, :]).reshape(T, PEER_HEADS, PEER_TOPK * PEER_TOPK)
    cidx = (i1[..., :, None] * PEER_NKEYS + i2[..., None, :]).reshape(T, PEER_HEADS, PEER_TOPK * PEER_TOPK)
    top_s, pos = lax.top_k(cand, PEER_TOPK)
    eidx = jnp.take_along_axis(cidx, pos, axis=-1)
    gate = jax.nn.softmax(top_s, axis=-1)
    nc = T // PEER_TOKEN_CHUNK
    xc = xt.reshape(nc, PEER_TOKEN_CHUNK, D)
    ec = eidx.reshape(nc, PEER_TOKEN_CHUNK, PEER_HEADS, PEER_TOPK)
    gc = gate.reshape(nc, PEER_TOKEN_CHUNK, PEER_HEADS, PEER_TOPK)

    def one(args):
        x_c, e_c, g_c = args
        u = expert_u[e_c]
        a = jnp.einsum('td,thkd->thk', x_c, u).astype(jnp.float32)
        w = (g_c * jax.nn.gelu(a, approximate=False)).astype(x_c.dtype)
        return jnp.einsum('thk,thkd->td', w, expert_v[e_c])

    out = lax.map(one, (xc, ec, gc))
    return out.reshape(B, S, D)

def setup_inputs(seed: int = 0) -> dict:
    key = jax.random.key(seed)
    ks = jax.random.split(key, 32)
    f32 = jnp.float32
    L = DEPTH

    def nrm(k, shape, scale):
        return jax.random.normal(k, shape, f32) * scale

    def gain(k, n):
        return 1.0 + 0.02 * jax.random.normal(k, (L, n), f32)

    offs = jax.random.randint(ks[2], (BATCH, 1), 0, 1024, dtype=jnp.int32)
    positions = offs + jnp.arange(SEQ, dtype=jnp.int32)[None, :]
    return {
        'x': nrm(ks[0], (BATCH, SEQ, D_MODEL), 1.0),
        'mem': nrm(ks[1], (BATCH, MEM_LEN, D_MODEL), 1.0),
        'positions': positions,
        'g_attn': gain(ks[3], D_MODEL),
        'w_in': nrm(ks[4], (L, D_MODEL, IN_COLS), D_MODEL ** -0.5),
        'g_q_a': gain(ks[5], MLA_Q_RANK),
        'w_uq': nrm(ks[6], (L, MLA_Q_RANK, MLA_HEADS * (MLA_NOPE + MLA_ROPE)), MLA_Q_RANK ** -0.5),
        'g_kv_a': gain(ks[7], MLA_KV_RANK),
        'w_ukv': nrm(ks[8], (L, MLA_KV_RANK, MLA_HEADS * (MLA_NOPE + MLA_V)), MLA_KV_RANK ** -0.5),
        'g_mla_o': gain(ks[9], MLA_OUT),
        'g_moba_o': gain(ks[10], MOBA_WIDTH),
        'w_out': nrm(ks[11], (L, MIX_WIDTH, D_MODEL), MIX_WIDTH ** -0.5),
        'g_cross': gain(ks[12], D_MODEL),
        'g_mem': gain(ks[13], D_MODEL),
        'w_cq': nrm(ks[14], (L, D_MODEL, D_MODEL), D_MODEL ** -0.5),
        'w_ck': nrm(ks[15], (L, D_MODEL, D_MODEL), D_MODEL ** -0.5),
        'w_cv': nrm(ks[16], (L, D_MODEL, D_MODEL), D_MODEL ** -0.5),
        'w_co': nrm(ks[17], (L, D_MODEL, D_MODEL), D_MODEL ** -0.5),
        'g_ffn': gain(ks[18], D_MODEL),
        'w_pq': nrm(ks[19], (L, D_MODEL, PEER_HEADS * PEER_DKEY), D_MODEL ** -0.5),
        'sub_keys1': nrm(ks[20], (L, PEER_NKEYS, PEER_DKEY // 2), (PEER_DKEY // 2) ** -0.5),
        'sub_keys2': nrm(ks[21], (L, PEER_NKEYS, PEER_DKEY // 2), (PEER_DKEY // 2) ** -0.5),
        'expert_u': nrm(ks[22], (L, PEER_N_EXPERTS, D_MODEL), D_MODEL ** -0.5),
        'expert_v': nrm(ks[23], (L, PEER_N_EXPERTS, D_MODEL), 0.5),
        'g_final': 1.0 + 0.02 * jax.random.normal(ks[24], (D_MODEL,), f32),
    }

def reference(x, mem, positions, g_attn, w_in, g_q_a, w_uq, g_kv_a, w_ukv, g_mla_o, g_moba_o,
              w_out, g_cross, g_mem, w_cq, w_ck, w_cv, w_co, g_ffn, w_pq, sub_keys1, sub_keys2,
              expert_u, expert_v, g_final):
    B, S, D = x.shape
    h = x
    for l in range(DEPTH):
        xn = rms_norm(h, g_attn[l])
        proj = xn @ w_in[l]
        c_q, c_kv, k_r, q_m, k_m, v_m = jnp.split(proj, IN_SPLITS, axis=-1)
        q = (rms_norm(c_q, g_q_a[l]) @ w_uq[l]).reshape(B, S, MLA_HEADS, MLA_NOPE + MLA_ROPE)
        q = jnp.concatenate([q[..., :MLA_NOPE], rope(q[..., MLA_NOPE:], positions)], axis=-1)
        kv = (rms_norm(c_kv, g_kv_a[l]) @ w_ukv[l]).reshape(B, S, MLA_HEADS, MLA_NOPE + MLA_V)
        k_nope, v = kv[..., :MLA_NOPE], kv[..., MLA_NOPE:]
        k_rope = rope(k_r.reshape(B, S, 1, MLA_ROPE), positions)
        k = jnp.concatenate([k_nope, jnp.broadcast_to(k_rope, (B, S, MLA_HEADS, MLA_ROPE))], axis=-1)
        o_mla = causal_block_attention(q.transpose(0, 2, 1, 3), k.transpose(0, 2, 1, 3),
                                       v.transpose(0, 2, 1, 3), (MLA_NOPE + MLA_ROPE) ** -0.5)
        qm = rope(q_m.reshape(B, S, MOBA_HEADS, MOBA_HEAD_DIM), positions).transpose(0, 2, 1, 3)
        km = rope(k_m.reshape(B, S, MOBA_HEADS, MOBA_HEAD_DIM), positions).transpose(0, 2, 1, 3)
        vm = v_m.reshape(B, S, MOBA_HEADS, MOBA_HEAD_DIM).transpose(0, 2, 1, 3)
        o_moba = moba_attention(qm, km, vm)
        mixed = jnp.concatenate([rms_norm(o_mla, g_mla_o[l]), rms_norm(o_moba, g_moba_o[l])], axis=-1)
        h = h + mixed @ w_out[l]
        h = h + memory_cross_attention(rms_norm(h, g_cross[l]), rms_norm(mem, g_mem[l]),
                                       w_cq[l], w_ck[l], w_cv[l], w_co[l])
        h = h + peer(rms_norm(h, g_ffn[l]), w_pq[l], sub_keys1[l], sub_keys2[l], expert_u[l], expert_v[l])
    return rms_norm(h, g_final)


_drawn_inputs = setup_inputs


def setup_inputs(seed=0):
    import zlib

    import numpy as np

    out = dict(_drawn_inputs(seed))
    spreads = {}
    factors = {'g_q_a': 2.67,
     'g_moba_o': 2.703,
     'g_cross': 8.0,
     'g_mem': 5.983,
     'g_final': 8.08,
     'g_ffn': 8.0}
    for name, (base, spread) in spreads.items():
        noise = np.random.default_rng([zlib.crc32(name.encode()), seed]).standard_normal(out[name].shape)
        drawn = base * np.exp(spread * noise) if base else spread * noise
        out[name] = __import__('jax').numpy.asarray(drawn.astype(out[name].dtype))
    for name, factor in factors.items():
        out[name] = (out[name] * factor).astype(out[name].dtype)
    return out
```

```python
import math
from contextlib import ExitStack

import concourse.bass as bass
import concourse.mybir as mybir

F32 = mybir.dt.float32
U32 = mybir.dt.uint32
I32 = mybir.dt.int32
ALU = mybir.AluOpType
ACT = mybir.ActivationFunctionType
AX = mybir.AxisListType.X

P = 128
EPS = 1e-6
SEQ, D = 256, 2048
T = SEQ // P
KB = D // P
Q_RANK, KV_RANK, ROPE = 512, 256, 64
HEADS, NOPE, HD = 8, 128, 128
QW = NOPE + ROPE
KVW = 2 * NOPE
C_W = Q_RANK + KV_RANK
QM0 = C_W + ROPE
KM0, VM0 = QM0 + HEADS * HD, QM0 + 2 * HEADS * HD
IN_COLS = QM0 + 3 * HEADS * HD
CROSS_HEADS = 4
CB = KB // CROSS_HEADS
ROUTER_HEADS, TOPK, NKEYS = 8, 16, 128
NCH = 512
RING, SLOT = 8, 4 * NCH
ROWS = 16
FREQS = ROPE // 2 + HD // 2
NEG = -1e30
LEAST = -3.0e38
G_ATTN, G_MEM, G_QA, G_KVA, G_MIX, G_CROSS, G_ROWS = 0, 16, 32, 36, 38, 54, 70

PI2_A = 6.25
PI2_B = math.floor((2 * math.pi - PI2_A) * 2048) / 2048
PI2_C = 2 * math.pi - PI2_A - PI2_B
ROUND = 12582912.0


class Own:

    def __init__(self, eng, sem, base=0):
        self.eng, self.sem, self.base, self.n = eng, sem, base, 0

    def mark(self, ins):
        ins.then_inc(self.sem, 1)
        self.n += 1

    def wait(self):
        self.eng.wait_ge(self.sem, self.base + self.n)

    def link(self, ins):
        self.mark(ins)
        self.wait()


def hold(eng, sem, value, passed):
    eng.wait_ge(sem, value)
    eng.sem_inc(passed, 1)


class Linear:

    def __init__(self, w, first_slot, first_chunk, kblocks=KB, pairs=D // NCH // 2):
        self.w, self.s0, self.c0, self.kb, self.pairs = w, first_slot, first_chunk, kblocks, pairs


def decoder_layer(nc, x, mem, positions, freqs, g_attn, w_in, g_q_a, w_uq, g_kv_a, w_ukv, g_mla_o,
                  g_moba_o, w_out, g_cross, g_mem, w_cq, w_ck, w_cv, w_co, g_ffn, w_pq, sub_keys1,
                  sub_keys2, expert_u, expert_v, g_final, out):
    ctx = ExitStack()
    with ctx:
        def sb(name, shape, dt=F32):
            return ctx.enter_context(nc.sbuf_tensor(name, shape, dt))

        def sem(name):
            return ctx.enter_context(nc.semaphore(name))

        def tiled(ap, t=T):
            return ap.rearrange("p (t n) -> p t n", t=t)

        arena = sb("arena", [P, RING * SLOT + T * IN_COLS + 4 * D + 9 * P])
        ring = arena[:, 0:RING * SLOT].rearrange("p (s k n) -> p s k n", s=RING, k=4)
        at = RING * SLOT
        proj = tiled(arena[:, at:at + T * IN_COLS])
        at += T * IN_COLS
        kv_up = tiled(arena[:, at:at + T * D])
        mem_rows = kv_up
        gain_wide = arena[:, at:at + D]
        at += T * D
        cross_v = tiled(arena[:, at:at + T * D])
        at += T * D
        q_stage = tiled(arena[:, at:at + T * QW])
        k_stage = tiled(arena[:, at + T * QW:at + T * QW + T * P])
        qm_stage = tiled(arena[:, at + T * (QW + P):at + T * (QW + 2 * P)])
        km_stage = tiled(arena[:, at + T * (QW + 2 * P):at + T * (QW + 3 * P)])
        expert_rows = arena[:, 0:ROWS * D].rearrange("p (s n) -> p s n", s=ROWS)

        h = sb("h", [P, T, D])
        xt = sb("xt", [P, KB, SEQ])
        mt = sb("mt", [P, KB, SEQ])
        scr = sb("scr", [P, T, D])
        flat = xt[:, :, :].rearrange("p k n -> p (k n)")
        mt_rows = tiled(mt[:, :, :].rearrange("p k n -> p (k n)"))
        rope_tmp = [flat[:, 1024 * n:1024 * n + 1024] for n in range(4)]
        qk_mla, qk_moba = flat[:, 0:512], flat[:, 512:1024]
        S3 = 3 * P
        sc = [flat[:, 1024 + S3 * n:1024 + S3 * n + S3] for n in range(2)]
        pr = [flat[:, 1792 + S3 * n:1792 + S3 * n + S3] for n in range(2)]
        prT = [flat[:, 2560 + S3 * n:2560 + S3 * n + S3] for n in range(2)]
        qr_T = flat[0:ROPE, 3328:3584]

        ident = sb("ident", [P, P])
        mask = sb("mask", [P, S3])
        gain_rows = sb("gain_rows", [G_ROWS, P])
        gains = sb("gains", [P, G_ROWS])
        pos_i = sb("pos_i", [T, P], I32)
        pos_f = sb("pos_f", [T, P])
        pos_t = sb("pos_t", [P, T])
        freq = sb("freq", [P, FREQS])
        sin = sb("sin", [P, T, FREQS])
        cos = sb("cos", [P, T, FREQS])
        ang = [flat[:, 200 * n:200 * n + T * FREQS].rearrange("p (t f) -> p t f", t=T) for n in range(2)]
        key_rows = arena[:, at:at + 2 * P].rearrange("p (k n) -> p k n", k=2)
        keys_T = sb("keys_T", [P, 2, NKEYS])
        kr_T = sb("kr_T", [ROPE, SEQ])
        ssq = sb("ssq", [P, 2 * T])
        mean = sb("mean", [P, 2 * T])
        root = sb("root", [P, 2 * T])
        rstd = sb("rstd", [P, 2 * T])
        mx = sb("mx", [P, 8])
        nmx = sb("nmx", [P, 8])
        den = sb("den", [P, 8])
        rden = sb("rden", [P, 8])
        o = [0]

        def small(n, dt=F32):
            o[0] += n
            ap = flat[:, o[0] - n:o[0]]
            return ap if dt == F32 else ap.bitcast(dt)

        half_s = small(2 * NKEYS).rearrange("p (k n) -> p k n", k=2)
        half_left = small(2 * NKEYS).rearrange("p (k n) -> p k n", k=2)
        top_v = small(2 * TOPK).rearrange("p (k n) -> p k n", k=2)
        top_i = small(2 * TOPK, U32).rearrange("p (k n) -> p k n", k=2)
        top_f = small(2 * TOPK).rearrange("p (k n) -> p k n", k=2)
        cand = small(TOPK * TOPK)
        cand_left = small(TOPK * TOPK)
        best = small(TOPK)
        spot = small(TOPK, U32)
        spot_ab = small(2 * TOPK, U32).rearrange("p (k n) -> p k n", k=2)
        spot_f = small(2 * TOPK).rearrange("p (k n) -> p k n", k=2)
        hot = [small(TOPK * TOPK).rearrange("p (k a) -> p k a", k=TOPK) for _ in range(2)]
        chosen = small(2 * TOPK).rearrange("p (k n) -> p k n", k=2)
        act_in = small(TOPK)
        act_out = small(TOPK)
        weight = small(TOPK)
        expert_id = [sb(f"expert_id{n}", [P, TOPK], U32) for n in range(2)]
        neg_best = [sb(f"neg_best{n}", [P, 1]) for n in range(2)]
        gate = [sb(f"gate{n}", [P, TOPK]) for n in range(2)]
        gate_sum = [sb(f"gate_sum{n}", [P, 1]) for n in range(2)]
        gate_inv = [sb(f"gate_inv{n}", [P, 1]) for n in range(2)]
        counts = sb("counts", [P, TOPK])

        bank = [ctx.enter_context(nc.psum_tensor(f"bank{n}", [P, NCH], F32)) for n in range(8)]

        x_landed, mem_landed, small_landed = sem("x_landed"), sem("mem_landed"), sem("small_landed")
        gain_landed, out_landed = sem("gain_landed"), sem("out_landed")
        weights_landed = [sem(f"weights_landed{n}") for n in range(RING)]
        weights_used = sem("weights_used")
        chunk_free = [sem(f"chunk_free{n}") for n in range(2)]
        turned = sem("turned")
        turned_free = [sem(f"turned_free{n}") for n in range(4)]
        made_ident, made_consts, pos_ready = sem("made_ident"), sem("made_consts"), sem("pos_ready")
        squares, means, roots, normed = sem("squares"), sem("means"), sem("roots"), sem("normed")
        angles_ready, sines_ready = sem("angles_ready"), sem("sines_ready")
        rotated = sem("rotated")
        residual = sem("residual")
        vec, act_own, pool_own = sem("vec"), sem("act_own"), sem("pool_own")
        vec_heads, vec_route = sem("vec_heads"), sem("vec_route")
        staged_a, staged_v = sem("staged_a"), sem("staged_v")
        head_T, head_T_a, head_T_v = sem("head_T"), sem("head_T_a"), sem("head_T_v")
        head_S, head_nmx, head_P = sem("head_S"), sem("head_nmx"), sem("head_P")
        head_PT, head_PT_a, head_PT_v = sem("head_PT"), sem("head_PT_a"), sem("head_PT_v")
        head_rden = sem("head_rden")
        head_O, head_O_a, head_O_v = sem("head_O"), sem("head_O_a"), sem("head_O_v")
        cr_S, cr_nmx, cr_P, cr_PT, cr_PTs, cr_O, cr_out = (sem("cr_" + n) for n in (
            "S", "nmx", "P", "PT", "PTs", "O", "out"))
        scored, scores_out_a, scores_out_v = sem("scored"), sem("scores_out_a"), sem("scores_out_v")
        half_staged, half_used = sem("half_staged"), sem("half_used")
        routed, passed = sem("routed"), sem("passed")
        gates_ready, activated = sem("gates_ready"), sem("activated")
        rows_landed = [sem(f"rows_landed{n}") for n in range(ROWS)]
        rows_used = sem("rows_used")

        L_in = Linear(w_in, 0, 0)
        L_ck = Linear(w_ck, 32, 8)
        L_cv = Linear(w_cv, 48, 12)
        UQ_S, UQ_C, UKV_S, UKV_C = 64, 16, 67, 19
        L_out = Linear(w_out, 69, 23)
        L_cq = Linear(w_cq, 85, 27)
        L_co = Linear(w_co, 101, 31)
        L_pq = Linear(w_pq, 117, 35)
        LAST_CHUNK_IN = IN_COLS - 7 * NCH

        def uses(c, parity):
            return (c + 1 - parity) // 2

        def chunks_out(eng, c):
            for parity in range(2):
                eng.wait_ge(chunk_free[parity], 2 * uses(c, parity))

        TG = {}
        n_groups = 0
        for name, groups in (("consts", 1), ("x", 8), ("mem", 8), ("k", 8), ("c", 3), ("kr", 1), ("mix", 8),
                             ("h1", 8), ("cq", 8), ("co", 8), ("h2", 8), ("pq", 8)):
            TG[name] = (n_groups, groups)
            n_groups += groups

        def group_bank(g):
            return bank[4 + g % 4]

        def groups_out(eng, g):
            for b in range(4):
                if (g + 3 - b) // 4:
                    eng.wait_ge(turned_free[b], (g + 3 - b) // 4)

        def bcast(g, n):
            return g.rearrange("(a n) -> a n", a=1).to_broadcast((n, g.shape[0]))

        def mix_half(t, n):
            half = scr[:, t, n * HEADS * P:(n + 1) * HEADS * P]
            return half if n else half.rearrange("p (h n) -> p h n", h=HEADS)

        mla_o = kv_up.rearrange("p t (h n) -> p t h n", h=HEADS)[:, :, :, 0:NOPE]
        moba_o = proj[:, :, QM0:KM0]
        mixed = [[mla_o[:, t, :, :], moba_o[:, t, :]] for t in range(T)]
        cross_p = [arena[:, RING * SLOT + SEQ * n:RING * SLOT + SEQ * (n + 1)] for n in range(2)]
        cross_pT_sb = [arena[:, RING * SLOT + SEQ * (n + 2):RING * SLOT + SEQ * (n + 3)] for n in range(2)]

        block = ctx.enter_context(nc.Block())

        @block.sync
        def _(sp):
            sp.dma_start(h[:, :, :], x.rearrange("(t p) n -> p t n", p=P)).then_inc(x_landed, 16)

            def load(slot, dst, src):
                sp.dma_start(dst, src).then_inc(weights_landed[slot], 16)

            def pair(L, i, cols=NCH):
                for j in range(8):
                    s = L.s0 + j
                    n = cols if j >= 4 else NCH
                    col = (2 * i + j // 4) * NCH
                    if not isinstance(i, int):
                        col = sp.snap(col)
                    if not isinstance(i, int) or s + 8 * i >= RING:
                        sp.wait_ge(weights_used, s + 8 * i - RING + 1)
                    load(s % RING, ring[:, s % RING, :, 0:n],
                         L.w[(j % 4) * 4 * P:(j % 4 + 1) * 4 * P, bass.ds(col, n)].rearrange("(k p) n -> p k n", p=P))

            def pairs(L):
                with sp.Fori(0, L.pairs) as i:
                    pair(L, i)

            pair(L_in, 0)
            with sp.Fori(1, 3) as i:
                pair(L_in, i)
            pair(L_in, 3, LAST_CHUNK_IN)
            pairs(L_ck)
            pairs(L_cv)
            for n in range(3):
                s = UQ_S + n
                sp.wait_ge(weights_used, s - RING + 1)
                load(s % RING, ring[:, s % RING, :, :],
                     w_uq[:, n * NCH:(n + 1) * NCH].rearrange("(k p) n -> p k n", p=P))
            for n in range(2):
                s = UKV_S + n
                sp.wait_ge(weights_used, s - RING + 1)
                load(s % RING, ring[:, s % RING, :, :].rearrange("p (k a) n -> p k (a n)", k=2),
                     w_ukv[:, n * 2 * NCH:(n + 1) * 2 * NCH].rearrange("(k p) n -> p k n", p=P))
            pairs(L_out)
            pairs(L_cq)
            sp.wait_ge(normed, 4)
            sp.dma_start(gain_wide, bcast(g_ffn, P)).then_inc(gain_landed, 16)
            pairs(L_co)
            pairs(L_pq)
            sp.wait_ge(scored, 8)
            sp.dma_start(flat[:, D:2 * D], bcast(g_final, P)).then_inc(gain_landed, 16)
            for t in range(T):
                sp.wait_ge(normed, 7 + t)
                sp.dma_start(out[t * P:(t + 1) * P, :], mt_rows[:, t, :]).then_inc(out_landed, 16)
            sp.wait_ge(out_landed, 16 * T)

        @block.gpsimd
        def _(pool):
            own = Own(pool, pool_own)
            pool.memset(ident[:, :], 0.0).then_inc(pool_own, 1)
            pool.memset(mask[:, :], 0.0).then_inc(pool_own, 1)
            pool.wait_ge(pool_own, 2)
            pool.affine_select(out=ident[:, :], in_=ident[:, :], compare_op=ALU.not_equal, fill=1.0, base=0,
                               pattern=[[-1, P]], channel_multiplier=1).then_inc(made_ident, 1)
            for b in (0, 2):
                pool.affine_select(out=mask[:, b * P:(b + 1) * P], in_=mask[:, b * P:(b + 1) * P],
                                   compare_op=ALU.is_ge, fill=NEG, base=0, pattern=[[-1, P]],
                                   channel_multiplier=1).then_inc(made_consts, 1)
            pool.iota(counts[:, :], pattern=[[1, TOPK]], base=0, channel_multiplier=0,
                      allow_small_or_imprecise_dtypes=True).then_inc(made_consts, 1)

            def gather(head, i, parity):
                for v, table in enumerate((expert_u, expert_v)):
                    if v == 0:
                        hold(pool, routed, head + 1, passed)
                    for k in range(TOPK):
                        if v or not isinstance(head, int) or head:
                            hold(pool, rows_used, head * 2 * TOPK + v * TOPK + k - ROWS + 1, passed)
                        pool.indirect_dma_start(
                            out=expert_rows[:, k, :], out_offset=None, in_=table[:, :],
                            in_offset=bass.IndirectOffsetOnAxis(ap=expert_id[parity][:, k:k + 1], axis=0),
                        ).then_inc(rows_landed[k], 16)

            gather(0, 0, 0)
            gather(1, 0, 1)
            with pool.Fori(1, ROUTER_HEADS * T // 2) as i:
                gather(2 * i, i, 0)
                gather(2 * i + 1, i, 1)

        @block.scalar
        def _(act):
            own = Own(act, act_own)
            for n, (row, g) in enumerate(((G_ATTN, g_attn), (G_MEM, g_mem), (G_QA, g_q_a), (G_KVA, g_kv_a),
                                          (G_MIX, g_mla_o), (G_MIX + 8, g_moba_o), (G_CROSS, g_cross))):
                rows = g.shape[0] // P
                act.dma_start(gain_rows[row:row + rows, :],
                              g.rearrange("(k p) -> k p", p=P)).then_inc(small_landed, 16)
            act.dma_start(pos_i[:, :], positions.rearrange("(t p) -> t p", p=P)).then_inc(small_landed, 16)
            act.dma_start(freq[:, :], bcast(freqs, P)).then_inc(small_landed, 16)
            act.dma_start(key_rows[:, 0, :], sub_keys1).then_inc(small_landed, 16)
            act.dma_start(key_rows[:, 1, :], sub_keys2).then_inc(small_landed, 16)
            act.dma_start(mem_rows, mem.rearrange("(t p) n -> p t n", p=P)).then_inc(mem_landed, 16)

            def squares_of(parts):
                for n, (src, junk) in enumerate(parts):
                    ins = act.activation(junk, src, ACT.Square, accum_out=ssq[:, n:n + 1])
                ins.then_inc(squares, 1)

            def root_of(job, n):
                act.wait_ge(means, job + 1)
                act.activation(root[:, 0:n], mean[:, 0:n], ACT.Sqrt).then_inc(roots, 1)

            def turn_out(name, dst, gain=None):
                g0, n = TG[name]
                for j in range(1, n, 2):
                    act.wait_ge(turned, g0 + j + 1)
                    src = group_bank(g0 + j)
                    if gain is None:
                        ins = act.copy(dst[:, 2 * j:2 * j + 2, :].rearrange("p k n -> p (k n)"), src[:, :])
                    else:
                        for k in range(2):
                            ins = act.activation(dst[:, 2 * j + k, :], src[:, k * SEQ:(k + 1) * SEQ], ACT.Copy,
                                                 scale=gains[:, gain + 2 * j + k:gain + 2 * j + k + 1])
                    ins.then_inc(turned_free[(g0 + j) % 4], 1)

            def chunk_out(c, slots, dst, n=NCH):
                act.wait_ge(weights_used, slots)
                act.copy(dst, bank[2 * (c % 2)][:, 0:n]).then_inc(chunk_free[c % 2], 1)

            def pair_out(L, i, dst, last=NCH):
                for cc in range(2):
                    n = last if cc else NCH
                    chunk_out(L.c0 + cc, L.s0 + 8 * i + 4 * cc + 4, dst(2 * i + cc, n), n)

            act.wait_ge(x_landed, 16)
            squares_of([(h[:, t, :], flat[:, t * D:(t + 1) * D]) for t in range(T)])
            root_of(0, T)
            act.wait_ge(mem_landed, 16)
            act.wait_ge(normed, 1)
            squares_of([(mem_rows[:, t, :], mt_rows[:, t, :]) for t in range(T)])
            act.wait_ge(turned_free[0], 1)
            turn_out("x", xt, G_ATTN)
            root_of(1, T)

            def proj_cols(c, n):
                return proj[:, 0, bass.ds(c * NCH, n)]

            pair_out(L_in, 0, proj_cols)
            with act.Fori(1, 3) as i:
                pair_out(L_in, i, proj_cols)
            pair_out(L_in, 3, proj_cols, LAST_CHUNK_IN)
            turn_out("mem", mt, G_MEM)
            chunks_out(act, 8)
            squares_of([(proj[:, t, a:b], cross_v[:, t, a:b])
                        for a, b in ((0, Q_RANK), (Q_RANK, C_W)) for t in range(T)])
            root_of(2, 2 * T)
            act.wait_ge(angles_ready, 1)
            act.activation(sin[:, :, :], ang[0], ACT.Sin)
            act.activation(cos[:, :, :], ang[1], ACT.Sin).then_inc(sines_ready, 1)

            def scr_cols(c, n):
                return scr[:, 0, bass.ds(c * NCH, n)]

            with act.Fori(0, 2) as i:
                pair_out(L_ck, i, scr_cols)
            with act.Fori(0, 2) as i:
                pair_out(L_cv, i, lambda c, n: cross_v[:, 0, bass.ds(c * NCH, n)])
            turn_out("k", mt)
            turn_out("c", xt, G_QA)
            act.wait_ge(turned, TG["k"][0] + 8)
            for n in range(3):
                chunk_out(UQ_C + n, UQ_S + n + 1, scr[:, 0, n * NCH:(n + 1) * NCH])
            for n in range(4):
                chunk_out(UKV_C + n, UKV_S + n // 2 + 1, kv_up[:, 0, n * NCH:(n + 1) * NCH])

            q_rows = scr[:, :, 0:HEADS * QW]
            chunks_out(act, L_out.c0)
            act.wait_ge(rotated, 4)

            def head(i):
                if not isinstance(i, int) or i:
                    hold(act, head_T, 3 * i, passed)
                act.copy(q_stage, q_rows[:, :, bass.ds(i * QW, QW)])
                act.copy(k_stage, kv_up[:, :, bass.ds(i * KVW, NOPE)]).then_inc(staged_a, 1)
                act.wait_ge(head_T, 3 * i + 2)
                act.copy(qk_mla, bank[4][:, :])
                act.copy(qr_T, bank[6][0:ROPE, 0:SEQ]).then_inc(head_T_a, 1)
                for m, scale in ((0, QW ** -0.5), (1, HD ** -0.5)):
                    act.wait_ge(head_nmx, 2 * i + m + 1)
                    for t in range(T):
                        a, b = (0, P) if t == 0 else (P, S3)
                        ins = act.activation(pr[m][:, a:b], sc[m][:, a:b], ACT.Exp, scale=scale,
                                             bias=nmx[:, 2 * m + t:2 * m + t + 1],
                                             accum_out=den[:, 2 * m + t:2 * m + t + 1])
                    ins.then_inc(head_P, 1)
                act.wait_ge(head_PT, 2 * i + 1)
                act.copy(prT[0], bank[0][:, 0:S3]).then_inc(head_PT_a, 1)
                act.wait_ge(head_rden, 2 * i + 1)
                hold(act, head_O, 2 * i + 1, passed)
                for t in range(T):
                    ins = act.activation(kv_up[:, t, bass.ds(i * KVW, NOPE)], bank[2][:, t * P:(t + 1) * P],
                                         ACT.Copy, scale=rden[:, t:t + 1])
                ins.then_inc(head_O_a, 1)

            head(0)
            with act.Fori(1, HEADS) as i:
                head(i)

            act.wait_ge(head_O_a, HEADS)
            act.wait_ge(head_O_v, HEADS)
            squares_of([(mixed[t][n], mix_half(t, n)) for n in range(2) for t in range(T)])
            root_of(3, 2 * T)
            turn_out("mix", xt, G_MIX)
            act.wait_ge(residual, 1)
            squares_of([(h[:, t, :], scr[:, t, :]) for t in range(T)])
            root_of(4, T)
            turn_out("h1", xt, G_CROSS)
            with act.Fori(0, 2) as i:
                pair_out(L_cq, i, scr_cols)
            turn_out("cq", xt)

            def cross_exp(g):
                b = g % 2
                act.wait_ge(cr_nmx, g + 1)
                if g >= 2:
                    act.wait_ge(cr_PT, g - 1)
                act.activation(cross_p[b], bank[b][:, 0:SEQ], ACT.Exp, scale=(D // CROSS_HEADS) ** -0.5,
                               bias=nmx[:, b:b + 1], accum_out=den[:, b:b + 1]).then_inc(cr_P, 1)

            def cross_pT(g):
                b = g % 2
                act.wait_ge(cr_PT, g + 1)
                if g >= 2:
                    act.wait_ge(cr_O, g - 1)
                act.copy(cross_pT_sb[b], bank[2 + b][:, 0:SEQ]).then_inc(cr_PTs, 1)

            for g in range(CROSS_HEADS * T + 1):
                if g < CROSS_HEADS * T:
                    cross_exp(g)
                if g >= 1:
                    cross_pT(g - 1)
            turn_out("co", xt)
            act.wait_ge(residual, 2)
            squares_of([(h[:, t, :], scr[:, t, :]) for t in range(T)])
            root_of(5, T)
            turn_out("h2", xt)
            with act.Fori(0, 2) as i:
                pair_out(L_pq, i, scr_cols)
            turn_out("pq", xt)
            for g in range(1, 8, 2):
                act.wait_ge(scored, g + 1)
                if g == 1:
                    groups_out(act, n_groups)
                act.copy(scr[:, g // 4, (g % 4) * NCH:(g % 4 + 1) * NCH],
                         bank[g % 4][:, :]).then_inc(scores_out_a, 1)

            heads = ROUTER_HEADS * T
            scores = scr[:, :, :].rearrange("p t n -> p (t n)")

            def stage(head):
                hold(act, half_used, head, passed)
                act.copy(half_s.rearrange("p k n -> p (k n)"),
                         scores[:, bass.ds(head * 2 * NKEYS, 2 * NKEYS)]).then_inc(half_staged, 1)

            def gates(head, parity):
                act.wait_ge(routed, head + 1)
                act.activation(gate[parity][:, :], best, ACT.Exp, bias=neg_best[parity][:, 0:1],
                               accum_out=gate_sum[parity][:, 0:1]).then_inc(gates_ready, 1)

            def gelu(head):
                act.wait_ge(rows_used, head * 2 * TOPK + TOPK)
                act.activation(act_out, act_in, ACT.Gelu).then_inc(activated, 1)

            act.wait_ge(scores_out_a, 4)
            act.wait_ge(scores_out_v, 4)
            act.copy(half_s.rearrange("p k n -> p (k n)"), scores[:, 0:2 * NKEYS]).then_inc(half_staged, 1)
            gates(0, 0)
            stage(1)

            with act.Fori(0, heads // 2 - 1) as i:
                for parity in range(2):
                    head_no = 2 * i + parity
                    gelu(head_no)
                    gates(head_no + 1, 1 - parity)
                    stage(head_no + 2)
            gelu(heads - 2)
            gates(heads - 1, 1)
            gelu(heads - 1)
            act.wait_ge(residual, 3)
            squares_of([(h[:, t, :], scr[:, t, :]) for t in range(T)])
            root_of(6, T)

        @block.vector
        def _(dve):
            own = Own(dve, vec)

            def mean_of(job, widths):
                dve.wait_ge(squares, job + 1)
                at = 0
                for n, w in widths:
                    ins = dve.tensor_scalar(mean[:, at:at + n], ssq[:, at:at + n], 1.0 / w, EPS, ALU.mult, ALU.add)
                    at += n
                ins.then_inc(means, 1)
                dve.wait_ge(roots, job + 1)
                own.link(dve.reciprocal(rstd[:, 0:at], root[:, 0:at]))

            def norm_rows(parts):
                for dst, src, n in parts:
                    ins = dve.tensor_scalar(dst, src, rstd[:, n:n + 1], None, ALU.mult)
                ins.then_inc(normed, 1)

            def turn_out(name, dst, gain=None):
                g0, n = TG[name]
                for j in range(0, n, 2):
                    dve.wait_ge(turned, g0 + j + 1)
                    to = dst[:, 2 * j:2 * j + 2, :]
                    src = group_bank(g0 + j)[:, :].rearrange("p (k n) -> p k n", k=2)
                    if gain is None:
                        ins = dve.tensor_copy(to, src)
                    else:
                        g = gains[:, gain + 2 * j:gain + 2 * j + 2].unsqueeze(2).to_broadcast((P, 2, SEQ))
                        ins = dve.tensor_tensor(to, src, g, ALU.mult)
                    ins.then_inc(turned_free[(g0 + j) % 4], 1)

            def chunk_out(c, slots, dst, n=NCH):
                dve.wait_ge(weights_used, slots)
                dve.tensor_copy(dst, bank[2 * (c % 2) + 1][:, 0:n]).then_inc(chunk_free[c % 2], 1)

            def pair_out(L, i, dst, last=NCH):
                for cc in range(2):
                    n = last if cc else NCH
                    chunk_out(L.c0 + cc, L.s0 + 8 * i + 4 * cc + 4, dst(2 * i + cc, n), n)

            def pair_add(L, i):
                for cc in range(2):
                    b = (L.c0 + cc) % 2
                    dve.wait_ge(weights_used, L.s0 + 8 * i + 4 * cc + 4)
                    for t in range(T):
                        to = h[:, t, bass.ds((2 * i + cc) * NCH, NCH)]
                        dve.tensor_tensor(to, to, bank[2 * b + t][:, :], ALU.add).then_inc(chunk_free[b], 1)

            dve.wait_ge(small_landed, 16 * 11)
            dve.tensor_copy(pos_f[:, :], pos_i[:, :]).then_inc(pos_ready, 1)
            mean_of(0, [(T, D)])
            norm_rows([(scr[:, t, :], h[:, t, :], t) for t in range(T)])
            dve.wait_ge(turned, 1)
            own.mark(dve.tensor_copy(gains[:, :], bank[4][:, 0:G_ROWS]))
            own.mark(dve.tensor_copy(pos_t[:, :], bank[4][:, 96:96 + T]))
            own.mark(dve.tensor_copy(keys_T[:, :, :], bank[4][:, 128:384].rearrange("p (k n) -> p k n", k=2)))
            own.wait()
            dve.sem_inc(turned_free[0], 1)
            turn_out("x", xt, G_ATTN)
            mean_of(1, [(T, D)])
            norm_rows([(mem_rows[:, t, :], mem_rows[:, t, :], t) for t in range(T)])

            def proj_cols(c, n):
                return proj[:, 1, bass.ds(c * NCH, n)]

            pair_out(L_in, 0, proj_cols)
            with dve.Fori(1, 3) as i:
                pair_out(L_in, i, proj_cols)
            pair_out(L_in, 3, proj_cols, LAST_CHUNK_IN)
            turn_out("mem", mt, G_MEM)
            chunks_out(dve, 8)

            a0, a1 = ang
            pos_b = pos_t[:, :].unsqueeze(2).to_broadcast((P, T, FREQS))
            freq_b = freq[:, :].unsqueeze(1).to_broadcast((P, T, FREQS))
            own.link(dve.tensor_tensor(a0, pos_b, freq_b, ALU.mult))
            for turns in (4096.0, 1.0):
                own.link(dve.tensor_scalar(a1, a0, 1.0 / (2 * math.pi * turns), ROUND, ALU.mult, ALU.add))
                own.link(dve.tensor_scalar(a1, a1, ROUND, None, ALU.subtract))
                for part in (PI2_A, PI2_B, PI2_C):
                    own.link(dve.scalar_tensor_tensor(out=a0, in0=a1, scalar=-part * turns, in1=a0,
                                                      op0=ALU.mult, op1=ALU.add))
            own.link(dve.tensor_scalar(a0, a0, 3.1415925, -3.1415925, ALU.min, ALU.max))
            own.link(dve.scalar_tensor_tensor(out=a1, in0=a0, scalar=-1.0, in1=a0, op0=ALU.mult, op1=ALU.max))
            dve.tensor_scalar(a1, a1, -1.0, math.pi / 2, ALU.mult, ALU.add).then_inc(angles_ready, 1)

            mean_of(2, [(T, Q_RANK), (T, KV_RANK)])
            norm_rows([(proj[:, t, a:b], proj[:, t, a:b], n * T + t)
                       for n, (a, b) in enumerate(((0, Q_RANK), (Q_RANK, C_W))) for t in range(T)])

            def rotate(ap, heads, f0, tmp, first=False):
                half = ap.shape[-1] // 2
                x1, x2 = ap[:, :, :, 0:half], ap[:, :, :, half:2 * half]
                c = cos[:, :, f0:f0 + half].unsqueeze(2).to_broadcast((P, T, heads, half))
                s = sin[:, :, f0:f0 + half].unsqueeze(2).to_broadcast((P, T, heads, half))
                tm = [x[:, 0:T * heads * half].rearrange("p (t h n) -> p t h n", t=T, h=heads) for x in tmp]
                own.mark(dve.tensor_tensor(tm[0], x1, c, ALU.mult))
                own.mark(dve.tensor_tensor(tm[1], x2, s, ALU.mult))
                own.mark(dve.tensor_tensor(tm[2], x1, s, ALU.mult))
                own.mark(dve.tensor_tensor(tm[3], x2, c, ALU.mult))
                own.wait()
                own.mark(dve.tensor_tensor(x1, tm[0], tm[1], ALU.subtract))
                own.link(dve.tensor_tensor(x2, tm[3], tm[2], ALU.add))
                dve.sem_inc(rotated, 1)

            dve.wait_ge(sines_ready, 1)
            rotate(proj[:, :, C_W:QM0].rearrange("p t (h n) -> p t h n", h=1), 1, 0, rope_tmp)
            with dve.Fori(0, 2) as i:
                pair_out(L_ck, i, lambda c, n: scr[:, 1, bass.ds(c * NCH, n)])
            rotate(proj[:, :, QM0:KM0].rearrange("p t (h n) -> p t h n", h=HEADS), HEADS, ROPE // 2, rope_tmp)
            rotate(proj[:, :, KM0:VM0].rearrange("p t (h n) -> p t h n", h=HEADS), HEADS, ROPE // 2, rope_tmp)
            with dve.Fori(0, 2) as i:
                pair_out(L_cv, i, lambda c, n: cross_v[:, 1, bass.ds(c * NCH, n)])
            turn_out("k", mt)
            turn_out("c", xt, G_QA)
            g = TG["kr"][0]
            dve.wait_ge(turned, g + 1)
            dve.tensor_copy(kr_T[:, :], group_bank(g)[0:ROPE, 0:SEQ]).then_inc(turned_free[g % 4], 1)
            q_rows = scr[:, :, 0:HEADS * QW]
            for n in range(3):
                chunk_out(UQ_C + n, UQ_S + n + 1, scr[:, 1, n * NCH:(n + 1) * NCH])
            chunks_out(dve, UKV_C)
            rotate(q_rows.rearrange("p t (h n) -> p t h n", h=HEADS)[:, :, :, NOPE:QW], HEADS, 0,
                   [x[:, 0:512] for x in (rope_tmp[2], rope_tmp[2][:, 512:1024], rope_tmp[3], rope_tmp[3][:, 512:1024])])
            for n in range(4):
                chunk_out(UKV_C + n, UKV_S + n // 2 + 1, kv_up[:, 1, n * NCH:(n + 1) * NCH])

            HEAD_STEPS = 6

            def head(i):
                step = Own(dve, vec_heads, HEAD_STEPS * i)
                if not isinstance(i, int) or i:
                    dve.wait_ge(head_T, 3 * i)
                dve.tensor_copy(qm_stage, proj[:, :, bass.ds(i * HD + QM0, HD)])
                dve.tensor_copy(km_stage, proj[:, :, bass.ds(i * HD + KM0, HD)]).then_inc(staged_v, 1)
                dve.wait_ge(head_T, 3 * i + 3)
                dve.tensor_copy(qk_moba, bank[5][:, :]).then_inc(head_T_v, 1)
                for m, scale in ((0, QW ** -0.5), (1, HD ** -0.5)):
                    dve.wait_ge(head_S, 2 * i + m + 1)
                    step.link(dve.tensor_tensor(sc[m], bank[7 if m else 3][:, 0:S3], mask[:, :], ALU.add))
                    for t in range(T):
                        a, b = (0, P) if t == 0 else (P, S3)
                        step.mark(dve.tensor_reduce(mx[:, 2 * m + t:2 * m + t + 1], sc[m][:, a:b], AX, ALU.max))
                    step.wait()
                    dve.tensor_scalar(nmx[:, 2 * m:2 * m + 2], mx[:, 2 * m:2 * m + 2], -scale, None,
                                      ALU.mult).then_inc(head_nmx, 1)
                for m in range(2):
                    dve.wait_ge(head_P, 2 * i + m + 1)
                    dve.reciprocal(rden[:, 2 * m:2 * m + 2], den[:, 2 * m:2 * m + 2]).then_inc(head_rden, 1)
                dve.wait_ge(head_PT, 2 * i + 2)
                dve.tensor_copy(prT[1], bank[1][:, 0:S3]).then_inc(head_PT_v, 1)
                dve.wait_ge(head_rden, 2 * i + 2)
                dve.wait_ge(head_O, 2 * i + 2)
                for t in range(T):
                    ins = dve.tensor_scalar(proj[:, t, bass.ds(i * HD + QM0, HD)], bank[1][:, t * P:(t + 1) * P],
                                            rden[:, 2 + t:3 + t], None, ALU.mult)
                ins.then_inc(head_O_v, 1)
                assert step.n == HEAD_STEPS

            chunks_out(dve, L_out.c0)
            head(0)
            with dve.Fori(1, HEADS) as i:
                head(i)
            mean_of(3, [(2 * T, HEADS * HD)])
            norm_rows([(mix_half(t, n), mixed[t][n], n * T + t) for n in range(2) for t in range(T)])
            turn_out("mix", xt, G_MIX)
            with dve.Fori(0, 2) as i:
                pair_add(L_out, i)
            chunks_out(dve, L_cq.c0)
            dve.sem_inc(residual, 1)
            mean_of(4, [(T, D)])
            norm_rows([(scr[:, t, :], h[:, t, :], t) for t in range(T)])
            turn_out("h1", xt, G_CROSS)
            with dve.Fori(0, 2) as i:
                pair_out(L_cq, i, lambda c, n: scr[:, 1, bass.ds(c * NCH, n)])
            turn_out("cq", xt)

            def cross_max(g):
                b = g % 2
                dve.wait_ge(cr_S, g + 1)
                if g >= 2:
                    dve.wait_ge(cr_P, g - 1)
                own.link(dve.tensor_reduce(mx[:, b:b + 1], bank[b][:, 0:SEQ], AX, ALU.max))
                dve.tensor_scalar(nmx[:, b:b + 1], mx[:, b:b + 1], -(D // CROSS_HEADS) ** -0.5, None,
                                  ALU.mult).then_inc(cr_nmx, 1)

            def cross_out(g):
                b, t, hd = g % 2, g % 2, g // 2
                dve.wait_ge(cr_P, g + 1)
                own.link(dve.reciprocal(rden[:, b:b + 1], den[:, b:b + 1]))
                dve.wait_ge(cr_O, g + 1)
                dve.tensor_scalar(scr[:, t, hd * NCH:(hd + 1) * NCH], bank[4 + b][:, :], rden[:, b:b + 1], None,
                                  ALU.mult).then_inc(cr_out, 1)

            n_g = CROSS_HEADS * T
            cross_max(0)
            cross_max(1)
            for g in range(n_g):
                cross_out(g)
                if g + 2 < n_g:
                    cross_max(g + 2)
            turn_out("co", xt)
            with dve.Fori(0, 2) as i:
                pair_add(L_co, i)
            chunks_out(dve, L_pq.c0)
            dve.sem_inc(residual, 1)
            mean_of(5, [(T, D)])
            dve.wait_ge(gain_landed, 16)
            for t in range(T):
                ins = dve.scalar_tensor_tensor(out=mt_rows[:, t, :], in0=h[:, t, :], scalar=rstd[:, t:t + 1],
                                               in1=gain_wide, op0=ALU.mult, op1=ALU.mult)
            ins.then_inc(normed, 1)
            turn_out("h2", xt)
            with dve.Fori(0, 2) as i:
                pair_out(L_pq, i, lambda c, n: scr[:, 1, bass.ds(c * NCH, n)])
            turn_out("pq", xt)
            for g in range(0, 8, 2):
                dve.wait_ge(scored, g + 1)
                if g == 0:
                    groups_out(dve, n_groups)
                dve.tensor_copy(scr[:, g // 4, (g % 4) * NCH:(g % 4 + 1) * NCH],
                                bank[g % 4][:, :]).then_inc(scores_out_v, 1)

            heads = ROUTER_HEADS * T

            def top16(r, values, left, tops, places):
                r.link(dve.max(tops[:, 0:8], values))
                r.mark(dve.match_replace(left, tops[:, 0:8], values, LEAST))
                r.mark(dve.max_index(places[:, 0:8], tops[:, 0:8], values))
                r.wait()
                r.link(dve.max(tops[:, 8:16], left))
                r.link(dve.max_index(places[:, 8:16], tops[:, 8:16], left))

            def route(head, parity):
                dve.sem_clear(vec_route)
                r = Own(dve, vec_route)
                hold(dve, half_staged, head + 1, passed)
                for s in range(2):
                    top16(r, half_s[:, s, :], half_left[:, s, :], top_v[:, s, :], top_i[:, s, :])
                dve.sem_inc(half_used, 1)
                r.mark(dve.tensor_copy(top_f[:, :, :], top_i[:, :, :]))
                r.mark(dve.tensor_tensor(cand.rearrange("p (a b) -> p a b", a=TOPK),
                                         top_v[:, 0, :].unsqueeze(2).to_broadcast((P, TOPK, TOPK)),
                                         top_v[:, 1, :].unsqueeze(1).to_broadcast((P, TOPK, TOPK)), ALU.add))
                r.wait()
                if not isinstance(head, int) or head:
                    hold(dve, gates_ready, head, passed)
                top16(r, cand, cand_left, best, spot)
                r.mark(dve.tensor_scalar(spot_ab[:, 0, :], spot, 4, None, ALU.logical_shift_right))
                r.mark(dve.tensor_scalar(spot_ab[:, 1, :], spot, TOPK - 1, None, ALU.bitwise_and))
                r.wait()
                r.link(dve.tensor_copy(spot_f[:, :, :], spot_ab[:, :, :]))
                for s in range(2):
                    r.mark(dve.tensor_tensor(hot[s], spot_f[:, s, :].unsqueeze(2).to_broadcast((P, TOPK, TOPK)),
                                             counts[:, :].unsqueeze(1).to_broadcast((P, TOPK, TOPK)), ALU.is_equal))
                r.wait()
                for s in range(2):
                    r.mark(dve.tensor_tensor(hot[s], hot[s],
                                             top_f[:, s, :].unsqueeze(1).to_broadcast((P, TOPK, TOPK)), ALU.mult))
                r.wait()
                for s in range(2):
                    r.mark(dve.tensor_reduce(chosen[:, s, :], hot[s], AX, ALU.add))
                r.wait()
                if not isinstance(head, int) or head >= 2:
                    dve.wait_ge(rows_used, (head - 1) * 2 * TOPK)
                r.mark(dve.tensor_scalar(neg_best[parity][:, :], best[:, 0:1], -1.0, None, ALU.mult))
                r.link(dve.scalar_tensor_tensor(out=expert_id[parity][:, :], in0=chosen[:, 0, :], scalar=float(NKEYS),
                                                in1=chosen[:, 1, :], op0=ALU.mult, op1=ALU.add))
                dve.sem_inc(routed, 1)

            def dots(head, t):
                for k in range(TOPK):
                    dve.wait_ge(rows_landed[k], 32 * head + 16)
                    dve.tensor_tensor_reduce(expert_rows[:, k, :], expert_rows[:, k, :], mt_rows[:, t, :], 1.0, 0.0,
                                             ALU.mult, ALU.add, act_in[:, k:k + 1]).then_inc(rows_used, 1)

            def combine(head, t, parity):
                dve.sem_clear(vec_route)
                r = Own(dve, vec_route)
                dve.wait_ge(gates_ready, head + 1)
                r.link(dve.reciprocal(gate_inv[parity][:, :], gate_sum[parity][:, :]))
                dve.wait_ge(activated, head + 1)
                r.link(dve.scalar_tensor_tensor(out=weight, in0=act_out, scalar=gate_inv[parity][:, 0:1],
                                                in1=gate[parity][:, :], op0=ALU.mult, op1=ALU.mult))
                for k in range(TOPK):
                    dve.wait_ge(rows_landed[k], 32 * head + 32)
                    dve.wait_ge(rows_used, head * 2 * TOPK + TOPK + k)
                    dve.scalar_tensor_tensor(out=h[:, t, :], in0=expert_rows[:, k, :], scalar=weight[:, k:k + 1],
                                             in1=h[:, t, :], op0=ALU.mult, op1=ALU.add).then_inc(rows_used, 1)

            dve.wait_ge(made_consts, 3)
            dve.wait_ge(scores_out_a, 4)
            dve.wait_ge(scores_out_v, 4)
            route(0, 0)
            for t in range(T):
                first = ROUTER_HEADS * t
                stop = ROUTER_HEADS // 2 - (t == T - 1)

                def pair(i, last=False):
                    for parity in range(2):
                        head_no = first + 2 * i + parity
                        dots(head_no, t)
                        if not (last and parity):
                            route(head_no + 1, 1 - parity)
                        combine(head_no, t, parity)

                if t == 0:
                    pair(0)
                with dve.Fori(1 if t == 0 else 0, stop) as i:
                    pair(i)
                if t == T - 1:
                    pair(stop, True)
            dve.wait_ge(rows_used, heads * 2 * TOPK)
            dve.sem_inc(residual, 1)
            mean_of(6, [(T, D)])
            dve.wait_ge(gain_landed, 32)
            for t in range(T):
                dve.scalar_tensor_tensor(out=mt_rows[:, t, :], in0=h[:, t, :], scalar=rstd[:, t:t + 1],
                                         in1=flat[:, D:2 * D], op0=ALU.mult, op1=ALU.mult).then_inc(normed, 1)

        @block.tensor
        def _(pe):
            def turn(name, rows):
                g0, n = TG[name]
                for j in range(n):
                    g = g0 + j
                    if g >= 4:
                        pe.wait_ge(turned_free[g % 4], g // 4)
                    for k in range(2):
                        for t in range(T):
                            ins = pe.transpose(group_bank(g)[:, (2 * k + t) * P:(2 * k + t + 1) * P],
                                               rows(t, 2 * j + k), ident[:, :])
                    ins.then_inc(turned, 1)

            def chunk(c, slots, src, n=NCH, free=None):
                if free is not None:
                    pe.wait_ge(chunk_free[c % 2], free)
                done = 0
                total = sum(len(kbs) for _, _, kbs, _ in slots)
                for slot, count, kbs, w in slots:
                    pe.wait_ge(weights_landed[slot], count)
                    for kk, kb in enumerate(kbs):
                        for t in range(T):
                            ins = pe.matmul(bank[2 * (c % 2) + t][:, 0:n], src[:, kb, t * P:(t + 1) * P], w(kk),
                                            start=(done == 0), stop=(done == total - 1))
                        done += 1
                    yield ins

            def pair(L, i, src, last=NCH, first=False):
                for cc in range(2):
                    c = L.c0 + cc
                    n = last if cc else NCH
                    slots = []
                    for j in range(4):
                        s = L.s0 + 4 * cc + j
                        slots.append((s % RING, 16 * (s // RING + 1) + 16 * i, range(4 * j, 4 * j + 4),
                                      lambda kk, sl=s % RING, n=n: ring[:, sl, kk, 0:n]))
                    for ins in chunk(c, slots, src, n, None if first else 2 * uses(c, c % 2) + 2 * i):
                        ins.then_inc(weights_used, 1)

            def linear(L, src):
                with pe.Fori(0, L.pairs) as i:
                    pair(L, i, src)

            pe.wait_ge(made_ident, 1)
            pe.wait_ge(small_landed, 16 * 11)
            pe.wait_ge(pos_ready, 1)
            pe.transpose(bank[4][:, 0:G_ROWS], gain_rows[:, :], ident[0:G_ROWS, 0:G_ROWS])
            pe.transpose(bank[4][:, 96:96 + T], pos_f[:, :], ident[0:T, 0:T])
            pe.transpose(bank[4][:, 128:256], key_rows[:, 0, :], ident[:, :])
            pe.transpose(bank[4][:, 256:384], key_rows[:, 1, :], ident[:, :]).then_inc(turned, 1)
            pe.wait_ge(normed, 1)
            turn("x", lambda t, kb: scr[:, t, kb * P:(kb + 1) * P])
            groups_out(pe, TG["mem"][0])
            pair(L_in, 0, xt, first=True)
            with pe.Fori(1, 3) as i:
                pair(L_in, i, xt)
            pair(L_in, 3, xt, LAST_CHUNK_IN)
            pe.wait_ge(normed, 2)
            turn("mem", lambda t, kb: mem_rows[:, t, kb * P:(kb + 1) * P])
            groups_out(pe, TG["k"][0])
            linear(L_ck, mt)
            linear(L_cv, mt)
            chunks_out(pe, L_cv.c0)
            turn("k", lambda t, kb: scr[:, t, kb * P:(kb + 1) * P])
            pe.wait_ge(normed, 3)
            pe.wait_ge(rotated, 3)
            turn("c", lambda t, kb: proj[:, t, kb * P:(kb + 1) * P])
            g = TG["kr"][0]
            pe.wait_ge(turned_free[g % 4], g // 4)
            pe.wait_ge(rotated, 1)
            for t in range(T):
                ins = pe.transpose(group_bank(g)[0:ROPE, t * P:(t + 1) * P], proj[:, t, C_W:QM0], ident[:, :])
            ins.then_inc(turned, 1)
            groups_out(pe, TG["mix"][0])
            for n in range(3):
                s, c = UQ_S + n, UQ_C + n
                for ins in chunk(c, [(s % RING, 16 * (s // RING + 1), range(4),
                                         lambda kk, sl=s % RING: ring[:, sl, kk, :])],
                                 xt, NCH, 2 * uses(c, c % 2)):
                    ins.then_inc(weights_used, 1)
            for n in range(4):
                s, c = UKV_S + n // 2, UKV_C + n
                for ins in chunk(c, [(s % RING, 16 * (s // RING + 1), range(4, 6),
                                         lambda kk, sl=s % RING, a=n % 2: ring[:, sl, 2 * kk + a, :])],
                                 xt, NCH, 2 * uses(c, c % 2)):
                    if n % 2:
                        ins.then_inc(weights_used, 1)

            chunks_out(pe, L_out.c0)
            pe.wait_ge(rotated, 4)
            pe.wait_ge(made_consts, 3)

            def head(i):
                for m, (staged, q, k) in enumerate(((staged_a, q_stage, k_stage), (staged_v, qm_stage, km_stage))):
                    pe.wait_ge(staged, i + 1)
                    if m == 0 and (not isinstance(i, int) or i):
                        pe.wait_ge(head_T_a, i)
                    if m == 1 and (not isinstance(i, int) or i):
                        pe.wait_ge(head_T_v, i)
                    for n, rows in enumerate((q, k)):
                        for t in range(T):
                            ins = pe.transpose(bank[4 + m][:, (2 * n + t) * P:(2 * n + t + 1) * P],
                                               rows[:, t, 0:P], ident[:, :])
                    ins.then_inc(head_T, 1)
                    if m == 0:
                        for t in range(T):
                            ins = pe.transpose(bank[6][0:ROPE, t * P:(t + 1) * P], q[:, t, P:QW], ident[:, :])
                        ins.then_inc(head_T, 1)
                for m, (qk, b, ready) in enumerate(((qk_mla, 3, head_T_a), (qk_moba, 7, head_T_v))):
                    pe.wait_ge(ready, i + 1)
                    if not isinstance(i, int) or i:
                        pe.wait_ge(head_nmx, 2 * i)
                    for t in range(T):
                        to = bank[b][:, 0:P] if t == 0 else bank[b][:, P:S3]
                        ins = pe.matmul(to, qk[:, t * P:(t + 1) * P], qk[:, SEQ:SEQ + (t + 1) * P],
                                        start=True, stop=(m == 1))
                        if m == 0:
                            ins = pe.matmul(to, qr_T[:, t * P:(t + 1) * P], kr_T[:, 0:(t + 1) * P],
                                            start=False, stop=True)
                    ins.then_inc(head_S, 1)
                for m, free in enumerate((head_PT_a, head_PT_v)):
                    pe.wait_ge(head_P, 2 * i + m + 1)
                    if not isinstance(i, int) or i:
                        pe.wait_ge(free, i)
                        if m:
                            pe.wait_ge(head_O_v, i)
                    for n in range(3):
                        ins = pe.transpose(bank[m][:, n * P:(n + 1) * P], pr[m][:, n * P:(n + 1) * P], ident[:, :])
                    ins.then_inc(head_PT, 1)
                if not isinstance(i, int) or i:
                    pe.wait_ge(head_O_a, i)
                for m, ready in enumerate((head_PT_a, head_PT_v)):
                    pe.wait_ge(ready, i + 1)
                    v = [kv_up[:, t, bass.ds(i * KVW + NOPE, NOPE)] if m == 0 else
                         proj[:, t, bass.ds(i * HD + VM0, HD)] for t in range(T)]
                    o_bank = bank[2 - m]
                    pe.matmul(o_bank[:, 0:P], prT[m][:, 0:P], v[0], start=True, stop=True)
                    pe.matmul(o_bank[:, P:SEQ], prT[m][:, P:2 * P], v[0], start=True, stop=False)
                    pe.matmul(o_bank[:, P:SEQ], prT[m][:, 2 * P:S3], v[1], start=False, stop=True).then_inc(head_O, 1)

            head(0)
            with pe.Fori(1, HEADS) as i:
                head(i)
            pe.wait_ge(head_O_a, HEADS)
            pe.wait_ge(head_O_v, HEADS)
            pe.wait_ge(normed, 4)
            turn("mix", lambda t, kb: scr[:, t, kb * P:(kb + 1) * P])
            groups_out(pe, TG["h1"][0])
            linear(L_out, xt)
            pe.wait_ge(normed, 5)
            turn("h1", lambda t, kb: scr[:, t, kb * P:(kb + 1) * P])
            groups_out(pe, TG["cq"][0])
            linear(L_cq, xt)
            chunks_out(pe, L_co.c0)
            turn("cq", lambda t, kb: scr[:, t, kb * P:(kb + 1) * P])
            groups_out(pe, TG["co"][0])
            n_g = CROSS_HEADS * T

            def cross_scores(g):
                hd, t = g // T, g % T
                if g >= 2:
                    pe.wait_ge(cr_P, g - 1)
                for k in range(CB):
                    ins = pe.matmul(bank[g % 2][:, 0:SEQ], xt[:, CB * hd + k, t * P:(t + 1) * P],
                                    mt[:, CB * hd + k, :], start=(k == 0), stop=(k == CB - 1))
                ins.then_inc(cr_S, 1)

            def cross_values(g):
                hd, b = g // T, g % 2
                pe.wait_ge(cr_P, g + 1)
                if g >= 2:
                    pe.wait_ge(cr_PTs, g - 1)
                for m in range(T):
                    ins = pe.transpose(bank[2 + b][:, m * P:(m + 1) * P], cross_p[b][:, m * P:(m + 1) * P], ident[:, :])
                ins.then_inc(cr_PT, 1)
                pe.wait_ge(cr_PTs, g + 1)
                if g >= 2:
                    pe.wait_ge(cr_out, g - 1)
                for m in range(T):
                    ins = pe.matmul(bank[4 + b][:, :], cross_pT_sb[b][:, m * P:(m + 1) * P],
                                    cross_v[:, m, hd * NCH:(hd + 1) * NCH], start=(m == 0), stop=(m == T - 1))
                ins.then_inc(cr_O, 1)

            cross_scores(0)
            for g in range(n_g):
                if g + 1 < n_g:
                    cross_scores(g + 1)
                cross_values(g)
            pe.wait_ge(cr_out, n_g)
            turn("co", lambda t, kb: scr[:, t, kb * P:(kb + 1) * P])
            groups_out(pe, TG["h2"][0])
            linear(L_co, xt)
            pe.wait_ge(normed, 6)
            turn("h2", lambda t, kb: mt_rows[:, t, kb * P:(kb + 1) * P])
            groups_out(pe, TG["pq"][0])
            linear(L_pq, xt)
            chunks_out(pe, L_pq.c0 + 4)
            turn("pq", lambda t, kb: scr[:, t, kb * P:(kb + 1) * P])
            groups_out(pe, n_groups)
            for g in range(8):
                t, h0 = g // 4, 2 * (g % 4)
                if g >= 4:
                    pe.wait_ge(scores_out_v if g % 2 == 0 else scores_out_a, (g - 4) // 2 + 1)
                for n in range(4):
                    ins = pe.matmul(bank[g % 4][:, n * P:(n + 1) * P], xt[:, 2 * h0 + n, t * P:(t + 1) * P],
                                    keys_T[:, n % 2, :], start=True, stop=True)
                ins.then_inc(scored, 1)


_NAMES = ['x', 'mem', 'positions', 'freqs', 'g_attn', 'w_in', 'g_q_a', 'w_uq', 'g_kv_a', 'w_ukv', 'g_mla_o',
          'g_moba_o', 'w_out', 'g_cross', 'g_mem', 'w_cq', 'w_ck', 'w_cv', 'w_co', 'g_ffn', 'w_pq', 'sub_keys1',
          'sub_keys2', 'expert_u', 'expert_v', 'g_final']


def kernel(**inputs):
    import numpy as _np
    import concourse.bacc as _bacc
    from concourse import mybir as _mybir
    from concourse.bass_utils import run_bass_kernel_spmd as _run

    nc = _bacc.Bacc("TRN2", target_bir_lowering=False, num_devices=1)
    freqs = _np.concatenate([
        _np.exp(_np.arange(n // 2, dtype=_np.float32) * _np.float32(-2.0 * math.log(10000.0) / n))
        for n in (ROPE, HD)]).astype(_np.float32)
    arrays, args = {}, []
    for name in _NAMES:
        a = freqs if name == 'freqs' else _np.asarray(inputs[name])
        if name not in ('freqs', 'g_final'):
            a = a[0]
        a = _np.ascontiguousarray(a)
        arrays[f"in_{name}_dram"] = a
        args.append(nc.dram_tensor(f"in_{name}_dram", a.shape, _mybir.dt.from_np(a.dtype), kind="ExternalInput").ap())
    args.append(nc.dram_tensor("out_dram", (SEQ, D), F32, kind="ExternalOutput").ap())
    decoder_layer(nc, *args)
    r = _run(nc, [arrays], core_ids=[0])
    return r.results[0]["out_dram"].reshape(1, SEQ, D)
```

```python
import math
from contextlib import ExitStack

import concourse.bass as bass
import concourse.mybir as mybir

F32 = mybir.dt.float32
F32R = mybir.dt.float32r
U32 = mybir.dt.uint32
I32 = mybir.dt.int32
ALU = mybir.AluOpType
ACT = mybir.ActivationFunctionType
AX = mybir.AxisListType.X

P = 128
EPS = 1e-6
SEQ, D = 256, 2048
T = SEQ // P
KB = D // P
Q_RANK, KV_RANK, ROPE = 512, 256, 64
HEADS, NOPE, HD = 8, 128, 128
QW = NOPE + ROPE
KVW = 2 * NOPE
C_W = Q_RANK + KV_RANK
QM0 = C_W + ROPE
KM0, VM0 = QM0 + HEADS * HD, QM0 + 2 * HEADS * HD
IN_COLS = QM0 + 3 * HEADS * HD
CROSS_HEADS = 4
CB = KB // CROSS_HEADS
ROUTER_HEADS, TOPK, NKEYS = 8, 16, 128
NCH = 512
UB = 2
RING = 4
PER_CHUNK = KB // UB
LEAD = 3
ROWS = 16
FREQS = ROPE // 2 + HD // 2
NEG = -1e30
LEAST = -3.0e38
G_ATTN, G_MEM, G_QA, G_KVA, G_MIX, G_CROSS, G_ROWS = 0, 16, 32, 36, 38, 54, 70

PI2_A = 6.25
PI2_B = math.floor((2 * math.pi - PI2_A) * 2048) / 2048
PI2_C = 2 * math.pi - PI2_A - PI2_B
ROUND = 12582912.0


class Own:

    def __init__(self, eng, sem, base=0):
        self.eng, self.sem, self.base, self.n = eng, sem, base, 0

    def mark(self, ins):
        ins.then_inc(self.sem, 1)
        self.n += 1

    def wait(self):
        self.eng.wait_ge(self.sem, self.base + self.n)

    def link(self, ins):
        self.mark(ins)
        self.wait()


def hold(eng, sem, value, passed):
    eng.wait_ge(sem, value)
    eng.sem_inc(passed, 1)


class Linear:

    def __init__(self, w, first_unit, first_chunk):
        self.w, self.u0, self.c0 = w, first_unit, first_chunk


PAIRS = D // NCH // 2


def decoder_layer(nc, x, mem, positions, freqs, g_attn, w_in, g_q_a, w_uq, g_kv_a, w_ukv, g_mla_o,
                  g_moba_o, w_out, g_cross, g_mem, w_cq, w_ck, w_cv, w_co, g_ffn, w_pq, sub_keys1,
                  sub_keys2, expert_u, expert_v, g_final, out):
    ctx = ExitStack()
    with ctx:
        def sb(name, shape, dt=F32):
            return ctx.enter_context(nc.sbuf_tensor(name, shape, dt))

        def sem(name):
            return ctx.enter_context(nc.semaphore(name))

        def tiled(ap, t=T):
            return ap.rearrange("p (t n) -> p t n", t=t)

        base = (nc.sbuf_base + 63) // 64 * 64
        XT, W_AT, RAW_AT = 0, 2 * KB * SEQ, 2 * KB * SEQ + 2 * RING * UB * NCH
        PROJ_AT = RAW_AT + RING * UB * NCH
        KV_AT = PROJ_AT + T * IN_COLS
        V_AT = KV_AT + T * D
        MAP_END = V_AT + T * D
        arena = sb("arena", [P, MAP_END])
        at_start = nc.alloc_sbuf_tensor_at

        xt_parts = [at_start(f"xt_{n}", [P, KB, SEQ], F32R, offset=base + 4 * (XT + k * KB * SEQ))
                    for k, n in enumerate(("hi", "lo"))]
        w_parts = [at_start(f"w_{n}", [P, RING, UB, NCH], F32R, offset=base + 4 * (W_AT + k * RING * UB * NCH))
                   for k, n in enumerate(("hi", "lo"))]
        raw = arena[:, RAW_AT:PROJ_AT].rearrange("p (s k n) -> p s k n", s=RING, k=UB)
        proj = tiled(arena[:, PROJ_AT:KV_AT])
        key_rows = arena[:, PROJ_AT:PROJ_AT + 2 * P].rearrange("p (k n) -> p k n", k=2)
        kv_up = tiled(arena[:, KV_AT:V_AT])
        mem_rows = kv_up
        gain_wide = arena[:, KV_AT:KV_AT + D]
        cross_v = tiled(arena[:, V_AT:MAP_END])
        work = arena[:, XT:XT + 2 * KB * SEQ]
        xt32 = arena[:, XT:XT + KB * SEQ].rearrange("p (k n) -> p k n", k=KB)
        STAGE = 4096
        q_stage = tiled(work[:, STAGE:STAGE + T * QW])
        k_stage = tiled(work[:, STAGE + T * QW:STAGE + T * QW + T * P])
        qm_stage = tiled(work[:, STAGE + T * (QW + P):STAGE + T * (QW + 2 * P)])
        km_stage = tiled(work[:, STAGE + T * (QW + 2 * P):STAGE + T * (QW + 3 * P)])
        expert_rows = arena[:, 0:ROWS * D].rearrange("p (s n) -> p s n", s=ROWS)
        after_rows = arena[:, ROWS * D:MAP_END]

        h = sb("h", [P, T, D])
        mt = sb("mt", [P, KB, SEQ])
        scr = sb("scr", [P, T, D])
        mt_flat = mt[:, :, :].rearrange("p k n -> p (k n)")
        mt_rows = tiled(mt_flat)
        rope_tmp = [mt_flat[:, 1024 * n:1024 * n + 1024] for n in range(4)]
        rope_tmp_q = [work[:, 2048 + 512 * n:2048 + 512 * n + 512] for n in range(4)]
        qk_mla, qk_moba = work[:, 0:512], work[:, 512:1024]
        S3 = 3 * P
        sc = [work[:, 1024 + S3 * n:1024 + S3 * n + S3] for n in range(2)]
        pr = [work[:, 1792 + S3 * n:1792 + S3 * n + S3] for n in range(2)]
        prT = [work[:, 2560 + S3 * n:2560 + S3 * n + S3] for n in range(2)]
        qr_T = work[0:ROPE, 3328:3584]

        ident = sb("ident", [P, P])
        mask = sb("mask", [P, S3])
        gain_rows = sb("gain_rows", [G_ROWS, P])
        gains = sb("gains", [P, G_ROWS])
        pos_i = sb("pos_i", [T, P], I32)
        pos_f = sb("pos_f", [T, P])
        pos_t = sb("pos_t", [P, T])
        freq = sb("freq", [P, FREQS])
        sin = sb("sin", [P, T, FREQS])
        cos = sb("cos", [P, T, FREQS])
        ang = [mt_flat[:, 200 * n:200 * n + T * FREQS].rearrange("p (t f) -> p t f", t=T) for n in range(2)]
        keys_T = sb("keys_T", [P, 2, NKEYS])
        kr_T = sb("kr_T", [ROPE, SEQ])
        ssq = sb("ssq", [P, 2 * T])
        mean = sb("mean", [P, 2 * T])
        root = sb("root", [P, 2 * T])
        rstd = sb("rstd", [P, 2 * T])
        mx = sb("mx", [P, 8])
        nmx = sb("nmx", [P, 8])
        den = sb("den", [P, 8])
        rden = sb("rden", [P, 8])
        o = [0]

        def small(n, dt=F32):
            o[0] += n
            ap = after_rows[:, o[0] - n:o[0]]
            return ap if dt == F32 else ap.bitcast(dt)

        half_s = small(2 * NKEYS).rearrange("p (k n) -> p k n", k=2)
        half_left = small(2 * NKEYS).rearrange("p (k n) -> p k n", k=2)
        top_v = small(2 * TOPK).rearrange("p (k n) -> p k n", k=2)
        top_i = small(2 * TOPK, U32).rearrange("p (k n) -> p k n", k=2)
        top_f = small(2 * TOPK).rearrange("p (k n) -> p k n", k=2)
        cand = small(TOPK * TOPK)
        cand_left = half_left.rearrange("p k n -> p (k n)")
        best = small(TOPK)
        spot = small(TOPK, U32)
        spot_ab = small(2 * TOPK, U32).rearrange("p (k n) -> p k n", k=2)
        spot_f = small(2 * TOPK).rearrange("p (k n) -> p k n", k=2)
        hot = [small(TOPK * TOPK).rearrange("p (k a) -> p k a", k=TOPK) for _ in range(2)]
        chosen = small(2 * TOPK).rearrange("p (k n) -> p k n", k=2)
        act_in = small(TOPK)
        act_out = small(TOPK)
        weight = small(TOPK)
        final_gain = small(D)
        assert o[0] <= MAP_END - ROWS * D
        expert_id = [sb(f"expert_id{n}", [P, TOPK], U32) for n in range(2)]
        neg_best = [sb(f"neg_best{n}", [P, 1]) for n in range(2)]
        gate = [sb(f"gate{n}", [P, TOPK]) for n in range(2)]
        gate_sum = [sb(f"gate_sum{n}", [P, 1]) for n in range(2)]
        gate_inv = [sb(f"gate_inv{n}", [P, 1]) for n in range(2)]
        counts = sb("counts", [P, TOPK])

        bank = [ctx.enter_context(nc.psum_tensor(f"bank{n}", [P, NCH], F32)) for n in range(8)]

        x_landed, mem_landed, small_landed = sem("x_landed"), sem("mem_landed"), sem("small_landed")
        gain_landed, out_landed = sem("gain_landed"), sem("out_landed")
        weights_landed = [sem(f"weights_landed{n}") for n in range(RING)]
        split_hi, split_lo = sem("split_hi"), sem("split_lo")
        weights_used = sem("weights_used")
        chunk_free = [sem(f"chunk_free{n}") for n in range(2)]
        turned = sem("turned")
        turned_free = [sem(f"turned_free{n}") for n in range(4)]
        turned_hi = sem("turned_hi")
        made_ident, made_consts, pos_ready = sem("made_ident"), sem("made_consts"), sem("pos_ready")
        squares, means, roots, normed = sem("squares"), sem("means"), sem("roots"), sem("normed")
        angles_ready, sines_ready = sem("angles_ready"), sem("sines_ready")
        rotated = sem("rotated")
        residual = sem("residual")
        vec, act_own, pool_own = sem("vec"), sem("act_own"), sem("pool_own")
        vec_heads, vec_route = sem("vec_heads"), sem("vec_route")
        staged_a, staged_v = sem("staged_a"), sem("staged_v")
        head_T, head_T_a, head_T_v = sem("head_T"), sem("head_T_a"), sem("head_T_v")
        head_S, head_nmx, head_P = sem("head_S"), sem("head_nmx"), sem("head_P")
        head_PT, head_PT_a, head_PT_v = sem("head_PT"), sem("head_PT_a"), sem("head_PT_v")
        head_rden = sem("head_rden")
        head_O, head_O_a, head_O_v = sem("head_O"), sem("head_O_a"), sem("head_O_v")
        cr_S, cr_nmx, cr_P, cr_PT, cr_PTs, cr_O, cr_out = (sem("cr_" + n) for n in (
            "S", "nmx", "P", "PT", "PTs", "O", "out"))
        scored, scores_out_a, scores_out_v = sem("scored"), sem("scores_out_a"), sem("scores_out_v")
        half_staged, half_used = sem("half_staged"), sem("half_used")
        routed, passed = sem("routed"), sem("passed")
        gates_ready, activated = sem("gates_ready"), sem("activated")
        rows_landed = [sem(f"rows_landed{n}") for n in range(ROWS)]
        rows_used = sem("rows_used")

        L_in = Linear(w_in, 0, 0)
        L_ck = Linear(w_ck, 64, 8)
        L_cv = Linear(w_cv, 96, 12)
        UQ_U, UQ_C = 128, 16
        UKV_U, UKV_C = 134, 19
        L_out = Linear(w_out, 138, 23)
        L_cq = Linear(w_cq, 170, 27)
        L_co = Linear(w_co, 202, 31)
        L_pq = Linear(w_pq, 234, 35)
        UNITS = 266
        LAST_CHUNK_IN = IN_COLS - 7 * NCH

        def uses(c, parity):
            return (c + 1 - parity) // 2

        def chunks_out(eng, c):
            for parity in range(2):
                eng.wait_ge(chunk_free[parity], 2 * uses(c, parity))

        TG = {}
        n_groups = 0
        for name, groups in (("consts", 1), ("x", 8), ("mem", 8), ("k", 8), ("c", 3), ("kr", 1), ("mix", 8),
                             ("h1", 8), ("cq", 8), ("co", 8), ("h2", 8), ("pq", 8)):
            TG[name] = (n_groups, groups)
            n_groups += groups

        def group_bank(g):
            return bank[4 + g % 4]

        def groups_out(eng, g):
            for b in range(4):
                if (g + 3 - b) // 4:
                    eng.wait_ge(turned_free[b], (g + 3 - b) // 4)

        def bcast(g, n):
            return g.rearrange("(a n) -> a n", a=1).to_broadcast((n, g.shape[0]))

        def mix_half(t, n):
            half = scr[:, t, n * HEADS * P:(n + 1) * HEADS * P]
            return half if n else half.rearrange("p (h n) -> p h n", h=HEADS)

        mla_o = kv_up.rearrange("p t (h n) -> p t h n", h=HEADS)[:, :, :, 0:NOPE]
        moba_o = proj[:, :, QM0:KM0]
        mixed = [[mla_o[:, t, :, :], moba_o[:, t, :]] for t in range(T)]
        cross_p = [arena[:, PROJ_AT + SEQ * n:PROJ_AT + SEQ * (n + 1)] for n in range(2)]
        cross_pT_sb = [arena[:, PROJ_AT + SEQ * (n + 2):PROJ_AT + SEQ * (n + 3)] for n in range(2)]

        block = ctx.enter_context(nc.Block())

        @block.sync
        def _(sp):
            sp.dma_start(h[:, :, :], x.rearrange("(t p) n -> p t n", p=P)).then_inc(x_landed, 16)

            def load(unit, i, w, kb, col, n=NCH):
                if not isinstance(i, int):
                    col = sp.snap(col)
                if not isinstance(i, int) or unit + 16 * i >= RING:
                    sp.wait_ge(split_lo, unit + 16 * i - RING + 1)
                sp.dma_start(raw[:, unit % RING, :, 0:n],
                             w[kb * P:(kb + UB) * P, bass.ds(col, n)].rearrange("(k p) n -> p k n", p=P)
                             ).then_inc(weights_landed[unit % RING], 16)

            def pair(L, i, last=NCH):
                for j in range(2 * PER_CHUNK):
                    cc = j // PER_CHUNK
                    load(L.u0 + j, i, L.w, j % PER_CHUNK * UB, (2 * i + cc) * NCH, last if cc else NCH)

            def pairs(L):
                with sp.Fori(0, PAIRS) as i:
                    pair(L, i)

            pair(L_in, 0)
            with sp.Fori(1, 3) as i:
                pair(L_in, i)
            pair(L_in, 3, LAST_CHUNK_IN)
            pairs(L_ck)
            pairs(L_cv)
            for n in range(3):
                for k in range(2):
                    load(UQ_U + 2 * n + k, 0, w_uq, k * UB, n * NCH)
            for n in range(4):
                load(UKV_U + n, 0, w_ukv, 0, n * NCH)
            pairs(L_out)
            pairs(L_cq)
            sp.wait_ge(normed, 4)
            sp.dma_start(gain_wide, bcast(g_ffn, P)).then_inc(gain_landed, 16)
            pairs(L_co)
            pairs(L_pq)
            sp.wait_ge(scored, 8)
            sp.dma_start(final_gain, bcast(g_final, P)).then_inc(gain_landed, 16)
            for t in range(T):
                sp.wait_ge(normed, 7 + t)
                sp.dma_start(out[t * P:(t + 1) * P, :], mt_rows[:, t, :]).then_inc(out_landed, 16)
            sp.wait_ge(out_landed, 16 * T)

        @block.gpsimd
        def _(pool):
            own = Own(pool, pool_own)
            pool.memset(ident[:, :], 0.0).then_inc(pool_own, 1)
            pool.memset(mask[:, :], 0.0).then_inc(pool_own, 1)
            pool.wait_ge(pool_own, 2)
            pool.affine_select(out=ident[:, :], in_=ident[:, :], compare_op=ALU.not_equal, fill=1.0, base=0,
                               pattern=[[-1, P]], channel_multiplier=1).then_inc(made_ident, 1)
            for b in (0, 2):
                pool.affine_select(out=mask[:, b * P:(b + 1) * P], in_=mask[:, b * P:(b + 1) * P],
                                   compare_op=ALU.is_ge, fill=NEG, base=0, pattern=[[-1, P]],
                                   channel_multiplier=1).then_inc(made_consts, 1)
            pool.iota(counts[:, :], pattern=[[1, TOPK]], base=0, channel_multiplier=0,
                      allow_small_or_imprecise_dtypes=True).then_inc(made_consts, 1)

            def gather(head, i, parity):
                for v, table in enumerate((expert_u, expert_v)):
                    if v == 0:
                        hold(pool, routed, head + 1, passed)
                    for k in range(TOPK):
                        if v or not isinstance(head, int) or head:
                            hold(pool, rows_used, head * 2 * TOPK + v * TOPK + k - ROWS + 1, passed)
                        pool.indirect_dma_start(
                            out=expert_rows[:, k, :], out_offset=None, in_=table[:, :],
                            in_offset=bass.IndirectOffsetOnAxis(ap=expert_id[parity][:, k:k + 1], axis=0),
                        ).then_inc(rows_landed[k], 16)

            gather(0, 0, 0)
            gather(1, 0, 1)
            with pool.Fori(1, ROUTER_HEADS * T // 2) as i:
                gather(2 * i, i, 0)
                gather(2 * i + 1, i, 1)

        @block.scalar
        def _(act):
            own = Own(act, act_own)
            for n, (row, g) in enumerate(((G_ATTN, g_attn), (G_MEM, g_mem), (G_QA, g_q_a), (G_KVA, g_kv_a),
                                          (G_MIX, g_mla_o), (G_MIX + 8, g_moba_o), (G_CROSS, g_cross))):
                rows = g.shape[0] // P
                act.dma_start(gain_rows[row:row + rows, :],
                              g.rearrange("(k p) -> k p", p=P)).then_inc(small_landed, 16)
            act.dma_start(pos_i[:, :], positions.rearrange("(t p) -> t p", p=P)).then_inc(small_landed, 16)
            act.dma_start(freq[:, :], bcast(freqs, P)).then_inc(small_landed, 16)
            act.dma_start(key_rows[:, 0, :], sub_keys1).then_inc(small_landed, 16)
            act.dma_start(key_rows[:, 1, :], sub_keys2).then_inc(small_landed, 16)
            act.dma_start(mem_rows, mem.rearrange("(t p) n -> p t n", p=P)).then_inc(mem_landed, 16)

            def squares_of(parts):
                for n, (src, junk) in enumerate(parts):
                    ins = act.activation(junk, src, ACT.Square, accum_out=ssq[:, n:n + 1])
                ins.then_inc(squares, 1)

            def root_of(job, n):
                act.wait_ge(means, job + 1)
                act.activation(root[:, 0:n], mean[:, 0:n], ACT.Sqrt).then_inc(roots, 1)

            def turn_out(name, dst):
                g0, n = TG[name]
                for j in range(1, n, 2):
                    act.wait_ge(turned, g0 + j + 1)
                    act.copy(dst[:, 2 * j:2 * j + 2, :].rearrange("p k n -> p (k n)"),
                             group_bank(g0 + j)[:, :]).then_inc(turned_free[(g0 + j) % 4], 1)

            def turn_hi(name, gain=None):
                g0, n = TG[name]
                hi = xt_parts[0]
                for j in range(n):
                    act.wait_ge(turned, g0 + j + 1)
                    src = group_bank(g0 + j)
                    if gain is None:
                        ins = act.copy(hi[:, 2 * j:2 * j + 2, :].rearrange("p k n -> p (k n)"), src[:, :])
                    else:
                        for k in range(2):
                            ins = act.activation(hi[:, 2 * j + k, :], src[:, k * SEQ:(k + 1) * SEQ], ACT.Copy,
                                                 scale=gains[:, gain + 2 * j + k:gain + 2 * j + k + 1])
                    ins.then_inc(turned_hi, 1)

            def split(unit, i=0, n=NCH):
                b = unit % RING
                act.wait_ge(weights_landed[b], 16 * (unit // RING + 1 + 4 * i))
                if not isinstance(i, int) or unit + 16 * i >= RING:
                    act.wait_ge(weights_used, unit + 16 * i - RING + 1)
                act.copy(w_parts[0][:, b, :, 0:n], raw[:, b, :, 0:n]).then_inc(split_hi, 1)

            def chunk_out(c, units, dst, n=NCH):
                act.wait_ge(weights_used, units)
                act.copy(dst, bank[2 * (c % 2)][:, 0:n]).then_inc(chunk_free[c % 2], 1)

            def pair_out(L, i, dst, last=NCH):
                for cc in range(2):
                    for j in range(PER_CHUNK):
                        u = L.u0 + LEAD + PER_CHUNK * cc + j
                        if isinstance(i, int):
                            u += 16 * i
                            whole = last == NCH or not 56 <= u < 64
                            if u < UNITS:
                                split(u, 0, NCH if whole else last)
                        else:
                            split(u, i)
                    if dst is not None:
                        n = last if cc else NCH
                        chunk_out(L.c0 + cc, L.u0 + 16 * i + PER_CHUNK * (cc + 1), dst(2 * i + cc, n), n)

            act.wait_ge(x_landed, 16)
            squares_of([(h[:, t, :], mt_rows[:, t, :]) for t in range(T)])
            root_of(0, T)
            act.wait_ge(mem_landed, 16)
            act.wait_ge(normed, 1)
            squares_of([(mem_rows[:, t, :], mt_rows[:, t, :]) for t in range(T)])
            act.wait_ge(turned_free[0], 1)
            turn_hi("x", G_ATTN)
            for u in range(LEAD):
                split(u)
            root_of(1, T)

            def proj_cols(c, n):
                return proj[:, 0, bass.ds(c * NCH, n)]

            pair_out(L_in, 0, proj_cols)
            with act.Fori(1, 3) as i:
                pair_out(L_in, i, proj_cols)
            pair_out(L_in, 3, proj_cols, LAST_CHUNK_IN)
            turn_hi("mem", G_MEM)
            chunks_out(act, 8)
            squares_of([(proj[:, t, a:b], cross_v[:, t, a:b])
                        for a, b in ((0, Q_RANK), (Q_RANK, C_W)) for t in range(T)])
            root_of(2, 2 * T)
            act.wait_ge(angles_ready, 1)
            act.activation(sin[:, :, :], ang[0], ACT.Sin)
            act.activation(cos[:, :, :], ang[1], ACT.Sin).then_inc(sines_ready, 1)

            def scr_cols(c, n):
                return scr[:, 0, bass.ds(c * NCH, n)]

            with act.Fori(0, PAIRS) as i:
                pair_out(L_ck, i, scr_cols)
            with act.Fori(0, PAIRS) as i:
                pair_out(L_cv, i, lambda c, n: cross_v[:, 0, bass.ds(c * NCH, n)])
            turn_out("k", mt)
            turn_hi("c", G_QA)
            for n in range(3):
                for k in range(2):
                    split(UQ_U + 2 * n + k + LEAD)
                chunk_out(UQ_C + n, UQ_U + 2 * n + 2, scr[:, 0, n * NCH:(n + 1) * NCH])
            for n in range(4):
                split(UKV_U + n + LEAD)
                chunk_out(UKV_C + n, UKV_U + n + 1, kv_up[:, 0, n * NCH:(n + 1) * NCH])

            q_rows = scr[:, :, 0:HEADS * QW]
            chunks_out(act, L_out.c0)
            act.wait_ge(rotated, 4)

            def head(i):
                if not isinstance(i, int) or i:
                    hold(act, head_T, 3 * i, passed)
                act.copy(q_stage, q_rows[:, :, bass.ds(i * QW, QW)])
                act.copy(k_stage, kv_up[:, :, bass.ds(i * KVW, NOPE)]).then_inc(staged_a, 1)
                act.wait_ge(head_T, 3 * i + 2)
                act.copy(qk_mla, bank[4][:, :])
                act.copy(qr_T, bank[6][0:ROPE, 0:SEQ]).then_inc(head_T_a, 1)
                for m, scale in ((0, QW ** -0.5), (1, HD ** -0.5)):
                    act.wait_ge(head_nmx, 2 * i + m + 1)
                    for t in range(T):
                        a, b = (0, P) if t == 0 else (P, S3)
                        ins = act.activation(pr[m][:, a:b], sc[m][:, a:b], ACT.Exp, scale=scale,
                                             bias=nmx[:, 2 * m + t:2 * m + t + 1],
                                             accum_out=den[:, 2 * m + t:2 * m + t + 1])
                    ins.then_inc(head_P, 1)
                act.wait_ge(head_PT, 2 * i + 1)
                act.copy(prT[0], bank[0][:, 0:S3]).then_inc(head_PT_a, 1)
                act.wait_ge(head_rden, 2 * i + 1)
                hold(act, head_O, 2 * i + 1, passed)
                for t in range(T):
                    ins = act.activation(kv_up[:, t, bass.ds(i * KVW, NOPE)], bank[2][:, t * P:(t + 1) * P],
                                         ACT.Copy, scale=rden[:, t:t + 1])
                ins.then_inc(head_O_a, 1)

            head(0)
            with act.Fori(1, HEADS) as i:
                head(i)

            act.wait_ge(head_O_a, HEADS)
            act.wait_ge(head_O_v, HEADS)
            squares_of([(mixed[t][n], mix_half(t, n)) for n in range(2) for t in range(T)])
            root_of(3, 2 * T)
            turn_hi("mix", G_MIX)
            with act.Fori(0, PAIRS) as i:
                pair_out(L_out, i, None)
            act.wait_ge(residual, 1)
            squares_of([(h[:, t, :], scr[:, t, :]) for t in range(T)])
            root_of(4, T)
            turn_hi("h1", G_CROSS)
            with act.Fori(0, PAIRS) as i:
                pair_out(L_cq, i, scr_cols)
            turn_out("cq", xt32)

            def cross_exp(g):
                b = g % 2
                act.wait_ge(cr_nmx, g + 1)
                if g >= 2:
                    act.wait_ge(cr_PT, g - 1)
                act.activation(cross_p[b], bank[b][:, 0:SEQ], ACT.Exp, scale=(D // CROSS_HEADS) ** -0.5,
                               bias=nmx[:, b:b + 1], accum_out=den[:, b:b + 1]).then_inc(cr_P, 1)

            def cross_pT(g):
                b = g % 2
                act.wait_ge(cr_PT, g + 1)
                if g >= 2:
                    act.wait_ge(cr_O, g - 1)
                act.copy(cross_pT_sb[b], bank[2 + b][:, 0:SEQ]).then_inc(cr_PTs, 1)

            for g in range(CROSS_HEADS * T + 1):
                if g < CROSS_HEADS * T:
                    cross_exp(g)
                if g >= 1:
                    cross_pT(g - 1)
            turn_hi("co")
            with act.Fori(0, PAIRS) as i:
                pair_out(L_co, i, None)
            act.wait_ge(residual, 2)
            squares_of([(h[:, t, :], scr[:, t, :]) for t in range(T)])
            root_of(5, T)
            turn_hi("h2")
            for i in range(PAIRS):
                pair_out(L_pq, i, scr_cols)
            turn_out("pq", xt32)
            for g in range(1, 8, 2):
                act.wait_ge(scored, g + 1)
                if g == 1:
                    groups_out(act, n_groups)
                act.copy(scr[:, g // 4, (g % 4) * NCH:(g % 4 + 1) * NCH],
                         bank[g % 4][:, :]).then_inc(scores_out_a, 1)

            heads = ROUTER_HEADS * T
            scores = scr[:, :, :].rearrange("p t n -> p (t n)")

            def stage(head):
                hold(act, half_used, head, passed)
                act.copy(half_s.rearrange("p k n -> p (k n)"),
                         scores[:, bass.ds(head * 2 * NKEYS, 2 * NKEYS)]).then_inc(half_staged, 1)

            def gates(head, parity):
                act.wait_ge(routed, head + 1)
                act.activation(gate[parity][:, :], best, ACT.Exp, bias=neg_best[parity][:, 0:1],
                               accum_out=gate_sum[parity][:, 0:1]).then_inc(gates_ready, 1)

            def gelu(head):
                act.wait_ge(rows_used, head * 2 * TOPK + TOPK)
                act.activation(act_out, act_in, ACT.Gelu).then_inc(activated, 1)

            act.wait_ge(scores_out_a, 4)
            act.wait_ge(scores_out_v, 4)
            act.copy(half_s.rearrange("p k n -> p (k n)"), scores[:, 0:2 * NKEYS]).then_inc(half_staged, 1)
            gates(0, 0)
            stage(1)

            with act.Fori(0, heads // 2 - 1) as i:
                for parity in range(2):
                    head_no = 2 * i + parity
                    gelu(head_no)
                    gates(head_no + 1, 1 - parity)
                    stage(head_no + 2)
            gelu(heads - 2)
            gates(heads - 1, 1)
            gelu(heads - 1)
            act.wait_ge(residual, 3)
            squares_of([(h[:, t, :], scr[:, t, :]) for t in range(T)])
            root_of(6, T)

        @block.vector
        def _(dve):
            own = Own(dve, vec)

            def mean_of(job, widths):
                dve.wait_ge(squares, job + 1)
                at = 0
                for n, w in widths:
                    ins = dve.tensor_scalar(mean[:, at:at + n], ssq[:, at:at + n], 1.0 / w, EPS, ALU.mult, ALU.add)
                    at += n
                ins.then_inc(means, 1)
                dve.wait_ge(roots, job + 1)
                own.link(dve.reciprocal(rstd[:, 0:at], root[:, 0:at]))

            def norm_rows(parts):
                for dst, src, n in parts:
                    ins = dve.tensor_scalar(dst, src, rstd[:, n:n + 1], None, ALU.mult)
                ins.then_inc(normed, 1)

            def turn_out(name, dst):
                g0, n = TG[name]
                for j in range(0, n, 2):
                    dve.wait_ge(turned, g0 + j + 1)
                    dve.tensor_copy(dst[:, 2 * j:2 * j + 2, :].rearrange("p k n -> p (k n)"),
                                    group_bank(g0 + j)[:, :]).then_inc(turned_free[(g0 + j) % 4], 1)

            hi_groups = [0]

            def turn_lo(name, gain=None):
                g0, n = TG[name]
                hi, lo = xt_parts
                for j in range(n):
                    hi_groups[0] += 1
                    dve.wait_ge(turned_hi, hi_groups[0])
                    src = group_bank(g0 + j)
                    for k in range(2):
                        if gain is None:
                            ins = dve.tensor_tensor(lo[:, 2 * j + k, :], src[:, k * SEQ:(k + 1) * SEQ],
                                                    hi[:, 2 * j + k, :].bitcast(F32), ALU.subtract)
                        else:
                            ins = dve.scalar_tensor_tensor(
                                out=lo[:, 2 * j + k, :], in0=src[:, k * SEQ:(k + 1) * SEQ],
                                scalar=gains[:, gain + 2 * j + k:gain + 2 * j + k + 1],
                                in1=hi[:, 2 * j + k, :].bitcast(F32), op0=ALU.mult, op1=ALU.subtract)
                    ins.then_inc(turned_free[(g0 + j) % 4], 1)

            def split(unit, i=0, n=NCH):
                b = unit % RING
                dve.wait_ge(split_hi, unit + 16 * i + 1)
                dve.tensor_tensor(w_parts[1][:, b, :, 0:n], raw[:, b, :, 0:n],
                                  w_parts[0][:, b, :, 0:n].bitcast(F32), ALU.subtract).then_inc(split_lo, 1)

            def chunk_out(c, units, dst, n=NCH):
                dve.wait_ge(weights_used, units)
                dve.tensor_copy(dst, bank[2 * (c % 2) + 1][:, 0:n]).then_inc(chunk_free[c % 2], 1)

            def chunk_add(c, units, col):
                dve.wait_ge(weights_used, units)
                for t in range(T):
                    to = h[:, t, bass.ds(col, NCH)]
                    dve.tensor_tensor(to, to, bank[2 * (c % 2) + t][:, :], ALU.add).then_inc(chunk_free[c % 2], 1)

            def pair_out(L, i, dst, last=NCH):
                for cc in range(2):
                    for j in range(PER_CHUNK):
                        u = L.u0 + LEAD + PER_CHUNK * cc + j
                        if isinstance(i, int):
                            u += 16 * i
                            whole = last == NCH or not 56 <= u < 64
                            if u < UNITS:
                                split(u, 0, NCH if whole else last)
                        else:
                            split(u, i)
                    units = L.u0 + 16 * i + PER_CHUNK * (cc + 1)
                    if dst is None:
                        chunk_add(L.c0 + cc, units, (2 * i + cc) * NCH)
                    else:
                        n = last if cc else NCH
                        chunk_out(L.c0 + cc, units, dst(2 * i + cc, n), n)

            dve.wait_ge(small_landed, 16 * 11)
            dve.tensor_copy(pos_f[:, :], pos_i[:, :]).then_inc(pos_ready, 1)
            mean_of(0, [(T, D)])
            norm_rows([(scr[:, t, :], h[:, t, :], t) for t in range(T)])
            dve.wait_ge(turned, 1)
            own.mark(dve.tensor_copy(gains[:, :], bank[4][:, 0:G_ROWS]))
            own.mark(dve.tensor_copy(pos_t[:, :], bank[4][:, 96:96 + T]))
            own.mark(dve.tensor_copy(keys_T[:, :, :], bank[4][:, 128:384].rearrange("p (k n) -> p k n", k=2)))
            own.wait()
            dve.sem_inc(turned_free[0], 1)
            turn_lo("x", G_ATTN)
            for u in range(LEAD):
                split(u)
            mean_of(1, [(T, D)])
            norm_rows([(mem_rows[:, t, :], mem_rows[:, t, :], t) for t in range(T)])

            def proj_cols(c, n):
                return proj[:, 1, bass.ds(c * NCH, n)]

            pair_out(L_in, 0, proj_cols)
            with dve.Fori(1, 3) as i:
                pair_out(L_in, i, proj_cols)
            pair_out(L_in, 3, proj_cols, LAST_CHUNK_IN)
            turn_lo("mem", G_MEM)
            chunks_out(dve, 8)

            a0, a1 = ang
            pos_b = pos_t[:, :].unsqueeze(2).to_broadcast((P, T, FREQS))
            freq_b = freq[:, :].unsqueeze(1).to_broadcast((P, T, FREQS))
            own.link(dve.tensor_tensor(a0, pos_b, freq_b, ALU.mult))
            for turns in (4096.0, 1.0):
                own.link(dve.tensor_scalar(a1, a0, 1.0 / (2 * math.pi * turns), ROUND, ALU.mult, ALU.add))
                own.link(dve.tensor_scalar(a1, a1, ROUND, None, ALU.subtract))
                for part in (PI2_A, PI2_B, PI2_C):
                    own.link(dve.scalar_tensor_tensor(out=a0, in0=a1, scalar=-part * turns, in1=a0,
                                                      op0=ALU.mult, op1=ALU.add))
            own.link(dve.tensor_scalar(a0, a0, 3.1415925, -3.1415925, ALU.min, ALU.max))
            own.link(dve.scalar_tensor_tensor(out=a1, in0=a0, scalar=-1.0, in1=a0, op0=ALU.mult, op1=ALU.max))
            dve.tensor_scalar(a1, a1, -1.0, math.pi / 2, ALU.mult, ALU.add).then_inc(angles_ready, 1)

            mean_of(2, [(T, Q_RANK), (T, KV_RANK)])
            norm_rows([(proj[:, t, a:b], proj[:, t, a:b], n * T + t)
                       for n, (a, b) in enumerate(((0, Q_RANK), (Q_RANK, C_W))) for t in range(T)])

            def rotate(ap, heads, f0, tmp, first=False):
                half = ap.shape[-1] // 2
                x1, x2 = ap[:, :, :, 0:half], ap[:, :, :, half:2 * half]
                c = cos[:, :, f0:f0 + half].unsqueeze(2).to_broadcast((P, T, heads, half))
                s = sin[:, :, f0:f0 + half].unsqueeze(2).to_broadcast((P, T, heads, half))
                tm = [x[:, 0:T * heads * half].rearrange("p (t h n) -> p t h n", t=T, h=heads) for x in tmp]
                own.mark(dve.tensor_tensor(tm[0], x1, c, ALU.mult))
                own.mark(dve.tensor_tensor(tm[1], x2, s, ALU.mult))
                own.mark(dve.tensor_tensor(tm[2], x1, s, ALU.mult))
                own.mark(dve.tensor_tensor(tm[3], x2, c, ALU.mult))
                own.wait()
                own.mark(dve.tensor_tensor(x1, tm[0], tm[1], ALU.subtract))
                own.link(dve.tensor_tensor(x2, tm[3], tm[2], ALU.add))
                dve.sem_inc(rotated, 1)

            dve.wait_ge(sines_ready, 1)
            rotate(proj[:, :, C_W:QM0].rearrange("p t (h n) -> p t h n", h=1), 1, 0, rope_tmp)
            with dve.Fori(0, PAIRS) as i:
                pair_out(L_ck, i, lambda c, n: scr[:, 1, bass.ds(c * NCH, n)])
            rotate(proj[:, :, QM0:KM0].rearrange("p t (h n) -> p t h n", h=HEADS), HEADS, ROPE // 2, rope_tmp)
            rotate(proj[:, :, KM0:VM0].rearrange("p t (h n) -> p t h n", h=HEADS), HEADS, ROPE // 2, rope_tmp)
            with dve.Fori(0, PAIRS) as i:
                pair_out(L_cv, i, lambda c, n: cross_v[:, 1, bass.ds(c * NCH, n)])
            turn_out("k", mt)
            turn_lo("c", G_QA)
            g = TG["kr"][0]
            dve.wait_ge(turned, g + 1)
            dve.tensor_copy(kr_T[:, :], group_bank(g)[0:ROPE, 0:SEQ]).then_inc(turned_free[g % 4], 1)
            q_rows = scr[:, :, 0:HEADS * QW]
            for n in range(3):
                for k in range(2):
                    split(UQ_U + 2 * n + k + LEAD)
                chunk_out(UQ_C + n, UQ_U + 2 * n + 2, scr[:, 1, n * NCH:(n + 1) * NCH])
            for n in range(4):
                split(UKV_U + n + LEAD)
                chunk_out(UKV_C + n, UKV_U + n + 1, kv_up[:, 1, n * NCH:(n + 1) * NCH])
            chunks_out(dve, L_out.c0)
            rotate(q_rows.rearrange("p t (h n) -> p t h n", h=HEADS)[:, :, :, NOPE:QW], HEADS, 0, rope_tmp_q)

            HEAD_STEPS = 6

            def head(i):
                step = Own(dve, vec_heads, HEAD_STEPS * i)
                if not isinstance(i, int) or i:
                    dve.wait_ge(head_T, 3 * i)
                dve.tensor_copy(qm_stage, proj[:, :, bass.ds(i * HD + QM0, HD)])
                dve.tensor_copy(km_stage, proj[:, :, bass.ds(i * HD + KM0, HD)]).then_inc(staged_v, 1)
                dve.wait_ge(head_T, 3 * i + 3)
                dve.tensor_copy(qk_moba, bank[5][:, :]).then_inc(head_T_v, 1)
                for m, scale in ((0, QW ** -0.5), (1, HD ** -0.5)):
                    dve.wait_ge(head_S, 2 * i + m + 1)
                    step.link(dve.tensor_tensor(sc[m], bank[7 if m else 3][:, 0:S3], mask[:, :], ALU.add))
                    for t in range(T):
                        a, b = (0, P) if t == 0 else (P, S3)
                        step.mark(dve.tensor_reduce(mx[:, 2 * m + t:2 * m + t + 1], sc[m][:, a:b], AX, ALU.max))
                    step.wait()
                    dve.tensor_scalar(nmx[:, 2 * m:2 * m + 2], mx[:, 2 * m:2 * m + 2], -scale, None,
                                      ALU.mult).then_inc(head_nmx, 1)
                for m in range(2):
                    dve.wait_ge(head_P, 2 * i + m + 1)
                    dve.reciprocal(rden[:, 2 * m:2 * m + 2], den[:, 2 * m:2 * m + 2]).then_inc(head_rden, 1)
                dve.wait_ge(head_PT, 2 * i + 2)
                dve.tensor_copy(prT[1], bank[1][:, 0:S3]).then_inc(head_PT_v, 1)
                dve.wait_ge(head_rden, 2 * i + 2)
                dve.wait_ge(head_O, 2 * i + 2)
                for t in range(T):
                    ins = dve.tensor_scalar(proj[:, t, bass.ds(i * HD + QM0, HD)], bank[1][:, t * P:(t + 1) * P],
                                            rden[:, 2 + t:3 + t], None, ALU.mult)
                ins.then_inc(head_O_v, 1)
                assert step.n == HEAD_STEPS

            head(0)
            with dve.Fori(1, HEADS) as i:
                head(i)
            mean_of(3, [(2 * T, HEADS * HD)])
            norm_rows([(mix_half(t, n), mixed[t][n], n * T + t) for n in range(2) for t in range(T)])
            turn_lo("mix", G_MIX)
            with dve.Fori(0, PAIRS) as i:
                pair_out(L_out, i, None)
            chunks_out(dve, L_cq.c0)
            dve.sem_inc(residual, 1)
            mean_of(4, [(T, D)])
            norm_rows([(scr[:, t, :], h[:, t, :], t) for t in range(T)])
            turn_lo("h1", G_CROSS)
            with dve.Fori(0, PAIRS) as i:
                pair_out(L_cq, i, lambda c, n: scr[:, 1, bass.ds(c * NCH, n)])
            turn_out("cq", xt32)

            def cross_max(g):
                b = g % 2
                dve.wait_ge(cr_S, g + 1)
                if g >= 2:
                    dve.wait_ge(cr_P, g - 1)
                own.link(dve.tensor_reduce(mx[:, b:b + 1], bank[b][:, 0:SEQ], AX, ALU.max))
                dve.tensor_scalar(nmx[:, b:b + 1], mx[:, b:b + 1], -(D // CROSS_HEADS) ** -0.5, None,
                                  ALU.mult).then_inc(cr_nmx, 1)

            def cross_out(g):
                b, t, hd = g % 2, g % 2, g // 2
                dve.wait_ge(cr_P, g + 1)
                own.link(dve.reciprocal(rden[:, b:b + 1], den[:, b:b + 1]))
                dve.wait_ge(cr_O, g + 1)
                dve.tensor_scalar(scr[:, t, hd * NCH:(hd + 1) * NCH], bank[4 + b][:, :], rden[:, b:b + 1], None,
                                  ALU.mult).then_inc(cr_out, 1)

            n_g = CROSS_HEADS * T
            cross_max(0)
            cross_max(1)
            for g in range(n_g):
                cross_out(g)
                if g + 2 < n_g:
                    cross_max(g + 2)
            turn_lo("co")
            with dve.Fori(0, PAIRS) as i:
                pair_out(L_co, i, None)
            chunks_out(dve, L_pq.c0)
            dve.sem_inc(residual, 1)
            mean_of(5, [(T, D)])
            dve.wait_ge(gain_landed, 16)
            for t in range(T):
                ins = dve.scalar_tensor_tensor(out=mt_rows[:, t, :], in0=h[:, t, :], scalar=rstd[:, t:t + 1],
                                               in1=gain_wide, op0=ALU.mult, op1=ALU.mult)
            ins.then_inc(normed, 1)
            turn_lo("h2")
            for i in range(PAIRS):
                pair_out(L_pq, i, lambda c, n: scr[:, 1, c * NCH:c * NCH + n])
            turn_out("pq", xt32)
            for g in range(0, 8, 2):
                dve.wait_ge(scored, g + 1)
                if g == 0:
                    groups_out(dve, n_groups)
                dve.tensor_copy(scr[:, g // 4, (g % 4) * NCH:(g % 4 + 1) * NCH],
                                bank[g % 4][:, :]).then_inc(scores_out_v, 1)

            heads = ROUTER_HEADS * T

            def top16(r, values, left, tops, places):
                r.link(dve.max(tops[:, 0:8], values))
                r.mark(dve.match_replace(left, tops[:, 0:8], values, LEAST))
                r.mark(dve.max_index(places[:, 0:8], tops[:, 0:8], values))
                r.wait()
                r.link(dve.max(tops[:, 8:16], left))
                r.link(dve.max_index(places[:, 8:16], tops[:, 8:16], left))

            def route(head, parity):
                dve.sem_clear(vec_route)
                r = Own(dve, vec_route)
                hold(dve, half_staged, head + 1, passed)
                for s in range(2):
                    top16(r, half_s[:, s, :], half_left[:, s, :], top_v[:, s, :], top_i[:, s, :])
                dve.sem_inc(half_used, 1)
                r.mark(dve.tensor_copy(top_f[:, :, :], top_i[:, :, :]))
                r.mark(dve.tensor_tensor(cand.rearrange("p (a b) -> p a b", a=TOPK),
                                         top_v[:, 0, :].unsqueeze(2).to_broadcast((P, TOPK, TOPK)),
                                         top_v[:, 1, :].unsqueeze(1).to_broadcast((P, TOPK, TOPK)), ALU.add))
                r.wait()
                if not isinstance(head, int) or head:
                    hold(dve, gates_ready, head, passed)
                top16(r, cand, cand_left, best, spot)
                r.mark(dve.tensor_scalar(spot_ab[:, 0, :], spot, 4, None, ALU.logical_shift_right))
                r.mark(dve.tensor_scalar(spot_ab[:, 1, :], spot, TOPK - 1, None, ALU.bitwise_and))
                r.wait()
                r.link(dve.tensor_copy(spot_f[:, :, :], spot_ab[:, :, :]))
                for s in range(2):
                    r.mark(dve.tensor_tensor(hot[s], spot_f[:, s, :].unsqueeze(2).to_broadcast((P, TOPK, TOPK)),
                                             counts[:, :].unsqueeze(1).to_broadcast((P, TOPK, TOPK)), ALU.is_equal))
                r.wait()
                for s in range(2):
                    r.mark(dve.tensor_tensor(hot[s], hot[s],
                                             top_f[:, s, :].unsqueeze(1).to_broadcast((P, TOPK, TOPK)), ALU.mult))
                r.wait()
                for s in range(2):
                    r.mark(dve.tensor_reduce(chosen[:, s, :], hot[s], AX, ALU.add))
                r.wait()
                if not isinstance(head, int) or head >= 2:
                    dve.wait_ge(rows_used, (head - 1) * 2 * TOPK)
                r.mark(dve.tensor_scalar(neg_best[parity][:, :], best[:, 0:1], -1.0, None, ALU.mult))
                r.link(dve.scalar_tensor_tensor(out=expert_id[parity][:, :], in0=chosen[:, 0, :], scalar=float(NKEYS),
                                                in1=chosen[:, 1, :], op0=ALU.mult, op1=ALU.add))
                dve.sem_inc(routed, 1)

            def dots(head, t):
                for k in range(TOPK):
                    dve.wait_ge(rows_landed[k], 32 * head + 16)
                    dve.tensor_tensor_reduce(expert_rows[:, k, :], expert_rows[:, k, :], mt_rows[:, t, :], 1.0, 0.0,
                                             ALU.mult, ALU.add, act_in[:, k:k + 1]).then_inc(rows_used, 1)

            def combine(head, t, parity):
                dve.sem_clear(vec_route)
                r = Own(dve, vec_route)
                dve.wait_ge(gates_ready, head + 1)
                r.link(dve.reciprocal(gate_inv[parity][:, :], gate_sum[parity][:, :]))
                dve.wait_ge(activated, head + 1)
                r.link(dve.scalar_tensor_tensor(out=weight, in0=act_out, scalar=gate_inv[parity][:, 0:1],
                                                in1=gate[parity][:, :], op0=ALU.mult, op1=ALU.mult))
                for k in range(TOPK):
                    dve.wait_ge(rows_landed[k], 32 * head + 32)
                    dve.wait_ge(rows_used, head * 2 * TOPK + TOPK + k)
                    dve.scalar_tensor_tensor(out=h[:, t, :], in0=expert_rows[:, k, :], scalar=weight[:, k:k + 1],
                                             in1=h[:, t, :], op0=ALU.mult, op1=ALU.add).then_inc(rows_used, 1)

            dve.wait_ge(made_consts, 3)
            dve.wait_ge(scores_out_a, 4)
            dve.wait_ge(scores_out_v, 4)
            route(0, 0)
            for t in range(T):
                first = ROUTER_HEADS * t
                stop = ROUTER_HEADS // 2 - (t == T - 1)

                def pair(i, last=False):
                    for parity in range(2):
                        head_no = first + 2 * i + parity
                        dots(head_no, t)
                        if not (last and parity):
                            route(head_no + 1, 1 - parity)
                        combine(head_no, t, parity)

                if t == 0:
                    pair(0)
                with dve.Fori(1 if t == 0 else 0, stop) as i:
                    pair(i)
                if t == T - 1:
                    pair(stop, True)
            dve.wait_ge(rows_used, heads * 2 * TOPK)
            dve.sem_inc(residual, 1)
            mean_of(6, [(T, D)])
            dve.wait_ge(gain_landed, 32)
            for t in range(T):
                dve.scalar_tensor_tensor(out=mt_rows[:, t, :], in0=h[:, t, :], scalar=rstd[:, t:t + 1],
                                         in1=final_gain, op0=ALU.mult, op1=ALU.mult).then_inc(normed, 1)

        @block.tensor
        def _(pe):
            def turn(name, rows):
                g0, n = TG[name]
                for j in range(n):
                    g = g0 + j
                    if g >= 4:
                        pe.wait_ge(turned_free[g % 4], g // 4)
                    for k in range(2):
                        for t in range(T):
                            ins = pe.transpose(group_bank(g)[:, (2 * k + t) * P:(2 * k + t + 1) * P],
                                               rows(t, 2 * j + k), ident[:, :])
                    ins.then_inc(turned, 1)

            def chunk(c, units, i=0, n=NCH, free=None, kb0=0):
                if free is not None:
                    pe.wait_ge(chunk_free[c % 2], free)
                hi, lo = xt_parts
                for at, u in enumerate(units):
                    pe.wait_ge(split_lo, u + 16 * i + 1)
                    w = [part[:, u % RING, :, 0:n] for part in w_parts]
                    for k in range(UB):
                        for t in range(T):
                            kb = kb0 + at * UB + k
                            to = bank[2 * (c % 2) + t][:, 0:n]
                            x_hi, x_lo = (part[:, kb, t * P:(t + 1) * P] for part in (hi, lo))
                            pe.matmul(to, x_hi, w[0][:, k, :], start=(at + k == 0), stop=False)
                            pe.matmul(to, x_hi, w[1][:, k, :], start=False, stop=False)
                            ins = pe.matmul(to, x_lo, w[0][:, k, :], start=False,
                                            stop=(at == len(units) - 1 and k == UB - 1))
                    ins.then_inc(weights_used, 1)

            def pair(L, i, last=NCH, first=False):
                for cc in range(2):
                    c, u = L.c0 + cc, L.u0 + PER_CHUNK * cc
                    chunk(c, range(u, u + PER_CHUNK), i, last if cc else NCH,
                          None if first else 2 * uses(c, c % 2) + 2 * i)

            def linear(L):
                with pe.Fori(0, PAIRS) as i:
                    pair(L, i)

            pe.wait_ge(made_ident, 1)
            pe.wait_ge(small_landed, 16 * 11)
            pe.wait_ge(pos_ready, 1)
            pe.transpose(bank[4][:, 0:G_ROWS], gain_rows[:, :], ident[0:G_ROWS, 0:G_ROWS])
            pe.transpose(bank[4][:, 96:96 + T], pos_f[:, :], ident[0:T, 0:T])
            pe.transpose(bank[4][:, 128:256], key_rows[:, 0, :], ident[:, :])
            pe.transpose(bank[4][:, 256:384], key_rows[:, 1, :], ident[:, :]).then_inc(turned, 1)
            pe.wait_ge(normed, 1)
            turn("x", lambda t, kb: scr[:, t, kb * P:(kb + 1) * P])
            groups_out(pe, TG["mem"][0])
            pair(L_in, 0, first=True)
            with pe.Fori(1, 3) as i:
                pair(L_in, i)
            pair(L_in, 3, LAST_CHUNK_IN)
            chunks_out(pe, L_ck.c0)
            pe.wait_ge(normed, 2)
            turn("mem", lambda t, kb: mem_rows[:, t, kb * P:(kb + 1) * P])
            groups_out(pe, TG["k"][0])
            linear(L_ck)
            linear(L_cv)
            chunks_out(pe, UQ_C)
            pe.wait_ge(rotated, 3)
            turn("k", lambda t, kb: scr[:, t, kb * P:(kb + 1) * P])
            pe.wait_ge(normed, 3)
            turn("c", lambda t, kb: proj[:, t, kb * P:(kb + 1) * P])
            g = TG["kr"][0]
            pe.wait_ge(turned_free[g % 4], g // 4)
            pe.wait_ge(rotated, 1)
            for t in range(T):
                ins = pe.transpose(group_bank(g)[0:ROPE, t * P:(t + 1) * P], proj[:, t, C_W:QM0], ident[:, :])
            ins.then_inc(turned, 1)
            groups_out(pe, TG["mix"][0])
            for n in range(3):
                c, u = UQ_C + n, UQ_U + 2 * n
                chunk(c, range(u, u + 2), free=2 * uses(c, c % 2))
            for n in range(4):
                c, u = UKV_C + n, UKV_U + n
                chunk(c, range(u, u + 1), free=2 * uses(c, c % 2), kb0=Q_RANK // P)

            chunks_out(pe, L_out.c0)
            pe.wait_ge(rotated, 4)
            pe.wait_ge(made_consts, 3)

            def head(i):
                for m, (staged, q, k) in enumerate(((staged_a, q_stage, k_stage), (staged_v, qm_stage, km_stage))):
                    pe.wait_ge(staged, i + 1)
                    if m == 0 and (not isinstance(i, int) or i):
                        pe.wait_ge(head_T_a, i)
                    if m == 1 and (not isinstance(i, int) or i):
                        pe.wait_ge(head_T_v, i)
                    for n, rows in enumerate((q, k)):
                        for t in range(T):
                            ins = pe.transpose(bank[4 + m][:, (2 * n + t) * P:(2 * n + t + 1) * P],
                                               rows[:, t, 0:P], ident[:, :])
                    ins.then_inc(head_T, 1)
                    if m == 0:
                        for t in range(T):
                            ins = pe.transpose(bank[6][0:ROPE, t * P:(t + 1) * P], q[:, t, P:QW], ident[:, :])
                        ins.then_inc(head_T, 1)
                for m, (qk, b, ready) in enumerate(((qk_mla, 3, head_T_a), (qk_moba, 7, head_T_v))):
                    pe.wait_ge(ready, i + 1)
                    if not isinstance(i, int) or i:
                        pe.wait_ge(head_nmx, 2 * i)
                    for t in range(T):
                        to = bank[b][:, 0:P] if t == 0 else bank[b][:, P:S3]
                        ins = pe.matmul(to, qk[:, t * P:(t + 1) * P], qk[:, SEQ:SEQ + (t + 1) * P],
                                        start=True, stop=(m == 1))
                        if m == 0:
                            ins = pe.matmul(to, qr_T[:, t * P:(t + 1) * P], kr_T[:, 0:(t + 1) * P],
                                            start=False, stop=True)
                    ins.then_inc(head_S, 1)
                for m, free in enumerate((head_PT_a, head_PT_v)):
                    pe.wait_ge(head_P, 2 * i + m + 1)
                    if not isinstance(i, int) or i:
                        pe.wait_ge(free, i)
                        if m:
                            pe.wait_ge(head_O_v, i)
                    for n in range(3):
                        ins = pe.transpose(bank[m][:, n * P:(n + 1) * P], pr[m][:, n * P:(n + 1) * P], ident[:, :])
                    ins.then_inc(head_PT, 1)
                if not isinstance(i, int) or i:
                    pe.wait_ge(head_O_a, i)
                for m, ready in enumerate((head_PT_a, head_PT_v)):
                    pe.wait_ge(ready, i + 1)
                    v = [kv_up[:, t, bass.ds(i * KVW + NOPE, NOPE)] if m == 0 else
                         proj[:, t, bass.ds(i * HD + VM0, HD)] for t in range(T)]
                    o_bank = bank[2 - m]
                    pe.matmul(o_bank[:, 0:P], prT[m][:, 0:P], v[0], start=True, stop=True)
                    pe.matmul(o_bank[:, P:SEQ], prT[m][:, P:2 * P], v[0], start=True, stop=False)
                    pe.matmul(o_bank[:, P:SEQ], prT[m][:, 2 * P:S3], v[1], start=False, stop=True).then_inc(head_O, 1)

            head(0)
            with pe.Fori(1, HEADS) as i:
                head(i)
            pe.wait_ge(head_O_a, HEADS)
            pe.wait_ge(head_O_v, HEADS)
            pe.wait_ge(normed, 4)
            turn("mix", lambda t, kb: scr[:, t, kb * P:(kb + 1) * P])
            groups_out(pe, TG["h1"][0])
            linear(L_out)
            pe.wait_ge(normed, 5)
            turn("h1", lambda t, kb: scr[:, t, kb * P:(kb + 1) * P])
            groups_out(pe, TG["cq"][0])
            linear(L_cq)
            chunks_out(pe, L_co.c0)
            turn("cq", lambda t, kb: scr[:, t, kb * P:(kb + 1) * P])
            groups_out(pe, TG["co"][0])
            n_g = CROSS_HEADS * T

            def cross_scores(g):
                hd, t = g // T, g % T
                if g >= 2:
                    pe.wait_ge(cr_P, g - 1)
                for k in range(CB):
                    ins = pe.matmul(bank[g % 2][:, 0:SEQ], xt32[:, CB * hd + k, t * P:(t + 1) * P],
                                    mt[:, CB * hd + k, :], start=(k == 0), stop=(k == CB - 1))
                ins.then_inc(cr_S, 1)

            def cross_values(g):
                hd, b = g // T, g % 2
                pe.wait_ge(cr_P, g + 1)
                if g >= 2:
                    pe.wait_ge(cr_PTs, g - 1)
                for m in range(T):
                    ins = pe.transpose(bank[2 + b][:, m * P:(m + 1) * P], cross_p[b][:, m * P:(m + 1) * P], ident[:, :])
                ins.then_inc(cr_PT, 1)
                pe.wait_ge(cr_PTs, g + 1)
                if g >= 2:
                    pe.wait_ge(cr_out, g - 1)
                for m in range(T):
                    ins = pe.matmul(bank[4 + b][:, :], cross_pT_sb[b][:, m * P:(m + 1) * P],
                                    cross_v[:, m, hd * NCH:(hd + 1) * NCH], start=(m == 0), stop=(m == T - 1))
                ins.then_inc(cr_O, 1)

            cross_scores(0)
            for g in range(n_g):
                if g + 1 < n_g:
                    cross_scores(g + 1)
                cross_values(g)
            pe.wait_ge(cr_out, n_g)
            turn("co", lambda t, kb: scr[:, t, kb * P:(kb + 1) * P])
            groups_out(pe, TG["h2"][0])
            linear(L_co)
            pe.wait_ge(normed, 6)
            turn("h2", lambda t, kb: mt_rows[:, t, kb * P:(kb + 1) * P])
            groups_out(pe, TG["pq"][0])
            linear(L_pq)
            chunks_out(pe, L_pq.c0 + 4)
            turn("pq", lambda t, kb: scr[:, t, kb * P:(kb + 1) * P])
            groups_out(pe, n_groups)
            for g in range(8):
                t, h0 = g // 4, 2 * (g % 4)
                if g >= 4:
                    pe.wait_ge(scores_out_v if g % 2 == 0 else scores_out_a, (g - 4) // 2 + 1)
                for n in range(4):
                    ins = pe.matmul(bank[g % 4][:, n * P:(n + 1) * P], xt32[:, 2 * h0 + n, t * P:(t + 1) * P],
                                    keys_T[:, n % 2, :], start=True, stop=True)
                ins.then_inc(scored, 1)


_NAMES = ['x', 'mem', 'positions', 'freqs', 'g_attn', 'w_in', 'g_q_a', 'w_uq', 'g_kv_a', 'w_ukv', 'g_mla_o',
          'g_moba_o', 'w_out', 'g_cross', 'g_mem', 'w_cq', 'w_ck', 'w_cv', 'w_co', 'g_ffn', 'w_pq', 'sub_keys1',
          'sub_keys2', 'expert_u', 'expert_v', 'g_final']


def kernel(**inputs):
    import numpy as _np
    import concourse.bacc as _bacc
    from concourse import mybir as _mybir
    from concourse.bass_utils import run_bass_kernel_spmd as _run

    nc = _bacc.Bacc("TRN2", target_bir_lowering=False, num_devices=1)
    freqs = _np.concatenate([
        _np.exp(_np.arange(n // 2, dtype=_np.float32) * _np.float32(-2.0 * math.log(10000.0) / n))
        for n in (ROPE, HD)]).astype(_np.float32)
    arrays, args = {}, []
    for name in _NAMES:
        a = freqs if name == 'freqs' else _np.asarray(inputs[name])
        if name not in ('freqs', 'g_final'):
            a = a[0]
        a = _np.ascontiguousarray(a)
        arrays[f"in_{name}_dram"] = a
        args.append(nc.dram_tensor(f"in_{name}_dram", a.shape, _mybir.dt.from_np(a.dtype), kind="ExternalInput").ap())
    args.append(nc.dram_tensor("out_dram", (SEQ, D), F32, kind="ExternalOutput").ap())
    decoder_layer(nc, *args)
    r = _run(nc, [arrays], core_ids=[0])
    return r.results[0]["out_dram"].reshape(1, SEQ, D)
```

```python
import math
from contextlib import ExitStack

import concourse.bass as bass
import concourse.mybir as mybir

F32 = mybir.dt.float32
F32R = mybir.dt.float32r
U32 = mybir.dt.uint32
I32 = mybir.dt.int32
ALU = mybir.AluOpType
ACT = mybir.ActivationFunctionType
AX = mybir.AxisListType.X

P = 128
EPS = 1e-6
SEQ, D = 256, 2048
T = SEQ // P
KB = D // P
Q_RANK, KV_RANK, ROPE = 512, 256, 64
HEADS, NOPE, HD = 8, 128, 128
QW = NOPE + ROPE
KVW = 2 * NOPE
C_W = Q_RANK + KV_RANK
QM0 = C_W + ROPE
KM0, VM0 = QM0 + HEADS * HD, QM0 + 2 * HEADS * HD
IN_COLS = QM0 + 3 * HEADS * HD
CROSS_HEADS = 4
CB = KB // CROSS_HEADS
ROUTER_HEADS, TOPK, NKEYS = 8, 16, 128
NCH = 512
UB = 2
RING = 4
PER_CHUNK = KB // UB
LEAD = 3
ROWS = 16
FREQS = ROPE // 2 + HD // 2
NEG = -1e30
LEAST = -3.0e38
G_ATTN, G_MEM, G_QA, G_KVA, G_MIX, G_CROSS, G_FFN, G_ROWS = 0, 16, 32, 36, 38, 54, 70, 86
N_X, N_MEM, N_C, N_MIX, N_H1, N_H2, N_OUT, N_COLS = 0, 2, 4, 8, 12, 14, 16, 19
NORMS = (N_X, N_MEM, N_C, N_MIX, N_H1, N_H2, N_OUT, N_OUT + 1)

PI2_A = 6.25
PI2_B = math.floor((2 * math.pi - PI2_A) * 2048) / 2048
PI2_C = 2 * math.pi - PI2_A - PI2_B
ROUND = 12582912.0


class Own:

    def __init__(self, eng, sem, base=0):
        self.eng, self.sem, self.base, self.n = eng, sem, base, 0

    def mark(self, ins):
        ins.then_inc(self.sem, 1)
        self.n += 1

    def wait(self):
        self.eng.wait_ge(self.sem, self.base + self.n)

    def link(self, ins):
        self.mark(ins)
        self.wait()


def hold(eng, sem, value, passed):
    eng.wait_ge(sem, value)
    eng.sem_inc(passed, 1)


class Linear:

    def __init__(self, w, first_unit, first_chunk):
        self.w, self.u0, self.c0 = w, first_unit, first_chunk


CHUNKS = D // NCH
PAIRS = CHUNKS // 2

BEFORE_IN = [("x", j) for j in range(LEAD + 1)]
BESIDE_IN = {**{(0, j - LEAD): [("x", j)] for j in range(LEAD + 1, KB // 2)}, (0, 5): [("consts", 0)]}
BESIDE_CV = {(n, 3): [("k", 2 * n), ("k", 2 * n + 1)] for n in range(4)}
BESIDE_OUT = {(n, 3): [("h1", 2 * n - 2), ("h1", 2 * n - 1)] for n in (1, 2, 3)}
BESIDE_CQ = {(0, 4): [("h1", 6), ("h1", 7)],
             (1, 2): [("q", 0), ("q", 1)], (1, 5): [("s", 0)],
             (2, 2): [("q", 2), ("q", 3)], (2, 3): [("p", 0)], (2, 5): [("o", 0)], (2, 6): [("s", 1)],
             (2, 7): [("o", 1)],
             (3, 2): [("q", 4), ("q", 5)], (3, 3): [("p", 1)], (3, 5): [("o", 2)], (3, 6): [("s", 2)],
             (3, 7): [("o", 3)]}
AFTER_CQ = [("q", 6), ("q", 7), ("p", 2), ("co", 0), ("s", 3), ("co", 1), ("o", 4), ("o", 5), ("co", 2), ("co", 3)]
BESIDE_CO = {(0, 1): [("p", 3)], (0, 3): [("o", 6), ("o", 7), ("co", 4), ("co", 5)], (0, 5): [("co", 6), ("co", 7)],
             **{(n, 3): [("h2", 2 * n - 2), ("h2", 2 * n - 1)] for n in (1, 2, 3)}}
BESIDE_PQ = {(0, 4): [("h2", 6), ("h2", 7)],
             **{(n, j): [(kind, 2 * n - 2), (kind, 2 * n - 1)] for n in (1, 2, 3) for j, kind in ((2, "rq"), (4, "rs"))}}
AFTER_PQ = [("rq", 6), ("rq", 7), ("rs", 6), ("rs", 7)]


def decoder_layer(nc, x, mem, positions, freqs, g_attn, w_in, g_q_a, w_uq, g_kv_a, w_ukv, g_mla_o,
                  g_moba_o, w_out, g_cross, g_mem, w_cq, w_ck, w_cv, w_co, g_ffn, w_pq, sub_keys1,
                  sub_keys2, expert_u, expert_v, g_final, out):
    ctx = ExitStack()
    with ctx:
        def sb(name, shape, dt=F32):
            return ctx.enter_context(nc.sbuf_tensor(name, shape, dt))

        def sem(name):
            return ctx.enter_context(nc.semaphore(name))

        def tiled(ap, t=T):
            return ap.rearrange("p (t n) -> p t n", t=t)

        base = (nc.sbuf_base + 63) // 64 * 64
        XT, W_AT, RAW_AT = 0, 2 * KB * SEQ, 2 * KB * SEQ + 2 * RING * UB * NCH
        PROJ_AT = RAW_AT + RING * UB * NCH
        KV_AT = PROJ_AT + T * IN_COLS
        V_AT = KV_AT + T * D
        MAP_END = V_AT + T * D
        FREE_AT = PROJ_AT + 2 * KB * SEQ
        assert FREE_AT + D + 2 * T * SEQ <= V_AT
        SLOTS = [10, 11, 14, 15, 9, 0, 2, 8, 5, 7, 1, 3, 4, 6, 12, 13]
        assert (RAW_AT, PROJ_AT, FREE_AT) == (8 * D, 10 * D, 14 * D)
        arena = sb("arena", [P, MAP_END])
        at_start = nc.alloc_sbuf_tensor_at

        xt_a, xt_b = ([at_start(f"xt_{m}_{n}", [P, KB, SEQ], F32R, offset=base + 4 * (at + k * KB * SEQ))
                       for k, n in enumerate(("hi", "lo"))] for m, at in (("a", XT), ("b", PROJ_AT)))
        w_parts = [at_start(f"w_{n}", [P, RING, UB, NCH], F32R, offset=base + 4 * (W_AT + k * RING * UB * NCH))
                   for k, n in enumerate(("hi", "lo"))]
        raw = arena[:, RAW_AT:PROJ_AT].rearrange("p (s k n) -> p s k n", s=RING, k=UB)
        proj = tiled(arena[:, PROJ_AT:KV_AT])
        key_rows = arena[:, PROJ_AT:PROJ_AT + 2 * P].rearrange("p (k n) -> p k n", k=2)
        kv_up = tiled(arena[:, KV_AT:V_AT])
        mem_rows = kv_up
        gain_wide = arena[:, FREE_AT:FREE_AT + D]
        cross_v = tiled(arena[:, V_AT:MAP_END])
        work = arena[:, XT:XT + 2 * KB * SEQ]
        xt_pq = arena[:, PROJ_AT + KB * SEQ:FREE_AT].rearrange("p (k n) -> p k n", k=KB)
        xt32 = arena[:, XT:XT + KB * SEQ].rearrange("p (k n) -> p k n", k=KB)
        STAGE = KB * SEQ + C_W // P * SEQ
        q_stage = tiled(work[:, STAGE:STAGE + T * QW])
        k_stage = tiled(work[:, STAGE + T * QW:STAGE + T * QW + T * P])
        qm_stage = tiled(work[:, STAGE + T * (QW + P):STAGE + T * (QW + 2 * P)])
        km_stage = tiled(work[:, STAGE + T * (QW + 2 * P):STAGE + T * (QW + 3 * P)])
        expert_rows = arena[:, 0:ROWS * D].rearrange("p (s n) -> p s n", s=ROWS)
        after_rows = arena[:, ROWS * D:MAP_END]

        h = sb("h", [P, T, D])
        mt = sb("mt", [P, KB, SEQ])
        scr = sb("scr", [P, T, D])
        mt_flat = mt[:, :, :].rearrange("p k n -> p (k n)")
        mt_rows = tiled(mt_flat)
        rope_tmp = [mt_flat[:, 1024 * n:1024 * n + 1024] for n in range(4)]
        rope_tmp_q = [work[:, 2048 + 512 * n:2048 + 512 * n + 512] for n in range(4)]
        qk_mla, qk_moba = work[:, 0:512], work[:, 512:1024]
        S3 = 3 * P
        sc = [work[:, 1024 + S3 * n:1024 + S3 * n + S3] for n in range(2)]
        pr = [work[:, 1792 + S3 * n:1792 + S3 * n + S3] for n in range(2)]
        prT = [work[:, 2560 + S3 * n:2560 + S3 * n + S3] for n in range(2)]
        QR_AT = STAGE + T * (QW + 3 * P)
        qr_T = work[0:ROPE, QR_AT:QR_AT + SEQ]

        ident = sb("ident", [P, P])
        mask = sb("mask", [P, S3])
        gain_rows = sb("gain_rows", [G_ROWS, P])
        gains = sb("gains", [P, G_ROWS])
        pos_i = sb("pos_i", [T, P], I32)
        pos_f = sb("pos_f", [T, P])
        pos_t = sb("pos_t", [P, T])
        freq = sb("freq", [P, FREQS])
        sin = sb("sin", [P, T, FREQS])
        cos = sb("cos", [P, T, FREQS])
        ang = [mt_flat[:, 200 * n:200 * n + T * FREQS].rearrange("p (t f) -> p t f", t=T) for n in range(3)]
        keys_T = sb("keys_T", [P, 2, NKEYS])
        kr_T = sb("kr_T", [ROPE, SEQ])
        ssq = sb("ssq", [P, N_COLS])
        mean = sb("mean", [P, N_COLS])
        root = sb("root", [P, N_COLS])
        rstd = sb("rstd", [P, N_COLS])
        mx = sb("mx", [P, 8])
        nmx = sb("nmx", [P, 8])
        den = sb("den", [P, 8])
        rden = sb("rden", [P, 8])
        o = [0]

        def small(n, dt=F32):
            o[0] += n
            ap = after_rows[:, o[0] - n:o[0]]
            return ap if dt == F32 else ap.bitcast(dt)

        half_s = small(2 * NKEYS).rearrange("p (k n) -> p k n", k=2)
        half_left = small(2 * NKEYS).rearrange("p (k n) -> p k n", k=2)
        top_v = small(2 * TOPK).rearrange("p (k n) -> p k n", k=2)
        top_i = small(2 * TOPK, U32).rearrange("p (k n) -> p k n", k=2)
        top_f = small(2 * TOPK).rearrange("p (k n) -> p k n", k=2)
        cand = small(TOPK * TOPK)
        cand_left = half_left.rearrange("p k n -> p (k n)")
        best = small(TOPK)
        spot = small(TOPK, U32)
        spot_ab = small(2 * TOPK, U32).rearrange("p (k n) -> p k n", k=2)
        spot_f = small(2 * TOPK).rearrange("p (k n) -> p k n", k=2)
        hot = [small(TOPK * TOPK).rearrange("p (k a) -> p k a", k=TOPK) for _ in range(2)]
        chosen = small(2 * TOPK).rearrange("p (k n) -> p k n", k=2)
        act_in = small(TOPK)
        act_out = small(TOPK)
        weight = small(TOPK)
        final_gain = small(D)
        assert o[0] <= MAP_END - ROWS * D
        expert_id = [sb(f"expert_id{n}", [P, TOPK], U32) for n in range(2)]
        neg_best = [sb(f"neg_best{n}", [P, 1]) for n in range(2)]
        gate = [sb(f"gate{n}", [P, TOPK]) for n in range(2)]
        gate_sum = [sb(f"gate_sum{n}", [P, 1]) for n in range(2)]
        gate_inv = [sb(f"gate_inv{n}", [P, 1]) for n in range(2)]
        counts = sb("counts", [P, TOPK])

        bank = [ctx.enter_context(nc.psum_tensor(f"bank{n}", [P, NCH], F32)) for n in range(8)]

        x_landed = [sem(f"x_landed{n}") for n in range(4)]
        mem_landed, small_landed, gains_landed = sem("mem_landed"), sem("small_landed"), sem("gains_landed")
        gain_landed, out_landed = sem("gain_landed"), sem("out_landed")
        weights_landed = [sem(f"weights_landed{n}") for n in range(RING)]
        split_hi, split_lo = sem("split_hi"), sem("split_lo")
        weights_used = sem("weights_used")
        chunk_free = [sem(f"chunk_free{n}") for n in range(2)]
        turned = sem("turned")
        turned_free = [sem(f"turned_free{n}") for n in range(4)]
        turned_hi = sem("turned_hi")
        made_ident, made_consts, pos_ready = sem("made_ident"), sem("made_consts"), sem("pos_ready")
        squares, means, roots, normed = sem("squares"), sem("means"), sem("roots"), sem("normed")
        angles_reduced, angles_ready, sines_ready = sem("angles_reduced"), sem("angles_ready"), sem("sines_ready")
        rstd_ready = sem("rstd_ready")
        rotated, rotated_q = sem("rotated"), sem("rotated_q")
        residual = sem("residual")
        vec, pool_own = sem("vec"), sem("pool_own")
        vec_heads, vec_route = sem("vec_heads"), sem("vec_route")
        staged_a, staged_v = sem("staged_a"), sem("staged_v")
        head_T, head_T_a, head_T_v = sem("head_T"), sem("head_T_a"), sem("head_T_v")
        head_S, head_nmx, head_P = sem("head_S"), sem("head_nmx"), sem("head_P")
        head_PT, head_PT_a, head_PT_v = sem("head_PT"), sem("head_PT_a"), sem("head_PT_v")
        head_rden = sem("head_rden")
        head_O, head_O_a, head_O_v = sem("head_O"), sem("head_O_a"), sem("head_O_v")
        cr_nmx = sem("cr_nmx")
        half_staged, half_used = sem("half_staged"), sem("half_used")
        routed, passed = sem("routed"), sem("passed")
        gates_ready, activated = sem("gates_ready"), sem("activated")
        rows_landed = [sem(f"rows_landed{n}") for n in range(ROWS)]
        rows_used = sem("rows_used")

        L_in = Linear(w_in, 0, 0)
        L_ck = Linear(w_ck, 64, 8)
        L_cv = Linear(w_cv, 96, 12)
        UQ_U, UQ_C = 128, 16
        UKV_U, UKV_C = 134, 19
        L_out = Linear(w_out, 138, 23)
        L_cq = Linear(w_cq, 170, 31)
        L_co = Linear(w_co, 202, 35)
        L_pq = Linear(w_pq, 234, 39)
        UNITS = 266
        LAST_CHUNK_IN = IN_COLS - 7 * NCH

        def uses(c, parity):
            return (c + 1 - parity) // 2

        def chunks_out(eng, c):
            for parity in range(2):
                eng.wait_ge(chunk_free[parity], 2 * uses(c, parity))

        TG = {}
        n_groups = 0
        for name, groups in (("gains", 1), ("x", 8), ("consts", 1), ("mem", 8), ("k", 8), ("c", 3), ("kr", 1), ("mix", 8)):
            TG[name] = (n_groups, groups)
            n_groups += groups

        STEP_G = {(kind, j): TG[kind][0] + j for kind in ("x", "consts", "k") for j in range(TG[kind][1])}
        for steps in (*BESIDE_OUT.values(), *BESIDE_CQ.values(), AFTER_CQ, *BESIDE_CO.values(),
                      *BESIDE_PQ.values(), AFTER_PQ):
            for step in steps:
                STEP_G[step] = n_groups
                n_groups += 1
        FIRST_STEP = STEP_G["h1", 0]

        def group_out(eng, g):
            eng.wait_ge(turned_free[g % 4], g // 4 + 1)

        def columns_out(eng, L, n, per=1):
            c = L.c0 + per * (n + 1) - 1
            eng.wait_ge(chunk_free[c % 2], 2 * uses(c + 1, c % 2))

        def group_bank(g):
            return bank[4 + g % 4]

        def groups_out(eng, g):
            for b in range(4):
                if (g + 3 - b) // 4:
                    eng.wait_ge(turned_free[b], (g + 3 - b) // 4)

        def bcast(g, n):
            return g.rearrange("(a n) -> a n", a=1).to_broadcast((n, g.shape[0]))

        def mix_half(t, n):
            half = scr[:, t, n * HEADS * P:(n + 1) * HEADS * P]
            return half if n else half.rearrange("p (h n) -> p h n", h=HEADS)

        mla_o = kv_up.rearrange("p t (h n) -> p t h n", h=HEADS)[:, :, :, 0:NOPE]
        moba_o = proj[:, :, QM0:KM0]
        mixed = [[mla_o[:, t, :, :], moba_o[:, t, :]] for t in range(T)]
        cross_p, cross_pT = (arena[:, FREE_AT + D + n:FREE_AT + D + n + T * SEQ] for n in (0, T * SEQ))

        def rotate(eng, own, ap, heads, f0, tmp, done):
            half = ap.shape[-1] // 2
            x1, x2 = ap[:, :, :, 0:half], ap[:, :, :, half:2 * half]
            c = cos[:, :, f0:f0 + half].unsqueeze(2).to_broadcast((P, T, heads, half))
            s = sin[:, :, f0:f0 + half].unsqueeze(2).to_broadcast((P, T, heads, half))
            tm = [x[:, 0:T * heads * half].rearrange("p (t h n) -> p t h n", t=T, h=heads) for x in tmp]
            own.mark(eng.tensor_tensor(tm[0], x1, c, ALU.mult))
            own.mark(eng.tensor_tensor(tm[1], x2, s, ALU.mult))
            own.mark(eng.tensor_tensor(tm[2], x1, s, ALU.mult))
            own.mark(eng.tensor_tensor(tm[3], x2, c, ALU.mult))
            own.wait()
            own.mark(eng.tensor_tensor(x1, tm[0], tm[1], ALU.subtract))
            own.link(eng.tensor_tensor(x2, tm[3], tm[2], ALU.add))
            eng.sem_inc(done, 1)

        def load_gains(eng, vectors):
            for row, g in vectors:
                eng.dma_start(gain_rows[row:row + g.shape[0] // P, :],
                              g.rearrange("(k p) -> k p", p=P)).then_inc(gains_landed, 16)

        block = ctx.enter_context(nc.Block())

        @block.sync
        def _(sp):
            def load(unit, i, w, kb, col, n=NCH):
                if not isinstance(i, int):
                    col = sp.snap(col)
                if not isinstance(i, int) or unit + 16 * i >= RING:
                    sp.wait_ge(split_lo, unit + 16 * i - RING + 1)
                sp.dma_start(raw[:, unit % RING, :, 0:n],
                             w[kb * P:(kb + UB) * P, bass.ds(col, n)].rearrange("(k p) n -> p k n", p=P)
                             ).then_inc(weights_landed[unit % RING], 16)

            def pair(L, i, last=NCH, first=0):
                for j in range(first, 2 * PER_CHUNK):
                    cc = j // PER_CHUNK
                    load(L.u0 + j, i, L.w, j % PER_CHUNK * UB, (2 * i + cc) * NCH, last if cc else NCH)

            def pairs(L):
                with sp.Fori(0, PAIRS) as i:
                    pair(L, i)

            for n in range(4):
                cols = slice(n * NCH, (n + 1) * NCH)
                sp.dma_start(h[:, :, cols], x[:, cols].rearrange("(t p) n -> p t n", p=P)).then_inc(x_landed[n], 16)
                if n == 0:
                    load_gains(sp, ((G_MIX, g_mla_o), (G_MIX + 8, g_moba_o), (G_CROSS, g_cross), (G_FFN, g_ffn)))
                load(n, 0, w_in, n * UB, 0)
            pair(L_in, 0, first=4)
            with sp.Fori(1, 3) as i:
                pair(L_in, i)
            pair(L_in, 3, LAST_CHUNK_IN)
            pairs(L_ck)
            pairs(L_cv)
            for n in range(3):
                for k in range(2):
                    load(UQ_U + 2 * n + k, 0, w_uq, k * UB, n * NCH)
            for n in range(4):
                load(UKV_U + n, 0, w_ukv, 0, n * NCH)
            pairs(L_out)
            pairs(L_cq)
            sp.wait_ge(turned, FIRST_STEP)
            sp.dma_start(gain_wide, bcast(g_ffn, P)).then_inc(gain_landed, 16)
            pairs(L_co)
            pairs(L_pq)
            sp.wait_ge(residual, 2)
            sp.dma_start(final_gain, bcast(g_final, P)).then_inc(gain_landed, 16)
            for n in range(2 * T):
                t, a = n // 2, n % 2 * D // 2
                sp.wait_ge(normed, n + 1)
                sp.dma_start(out[t * P:(t + 1) * P, a:a + D // 2], mt_rows[:, t, a:a + D // 2]).then_inc(out_landed, 16)
            sp.wait_ge(out_landed, 16 * 2 * T)

        @block.gpsimd
        def _(pool):
            own = Own(pool, pool_own, 2)
            pool.memset(ident[:, :], 0.0).then_inc(pool_own, 1)
            pool.memset(mask[:, :], 0.0).then_inc(pool_own, 1)
            pool.wait_ge(pool_own, 2)
            pool.affine_select(out=ident[:, :], in_=ident[:, :], compare_op=ALU.not_equal, fill=1.0, base=0,
                               pattern=[[-1, P]], channel_multiplier=1).then_inc(made_ident, 1)
            for b in (0, 2):
                pool.affine_select(out=mask[:, b * P:(b + 1) * P], in_=mask[:, b * P:(b + 1) * P],
                                   compare_op=ALU.is_ge, fill=NEG, base=0, pattern=[[-1, P]],
                                   channel_multiplier=1).then_inc(made_consts, 1)
            pool.iota(counts[:, :], pattern=[[1, TOPK]], base=0, channel_multiplier=0,
                      allow_small_or_imprecise_dtypes=True).then_inc(made_consts, 1)

            pool.wait_ge(small_landed, 16 * 4)
            pool.wait_ge(turned_free[TG["consts"][0] % 4], TG["consts"][0] // 4 + 1)
            a0, a1, a2 = ang
            pos_b = pos_t[:, :].unsqueeze(2).to_broadcast((P, T, FREQS))
            freq_b = freq[:, :].unsqueeze(1).to_broadcast((P, T, FREQS))
            own.link(pool.tensor_tensor(a0, pos_b, freq_b, ALU.mult))
            for turns in (4096.0, 1.0):
                own.link(pool.tensor_scalar(a1, a0, 1.0 / (2 * math.pi * turns), ROUND, ALU.mult, ALU.add))
                own.link(pool.tensor_scalar(a1, a1, ROUND, None, ALU.subtract))
                for part in (PI2_A, PI2_B, PI2_C):
                    own.link(pool.tensor_scalar(a2, a1, -part * turns, None, ALU.mult))
                    own.link(pool.tensor_tensor(a0, a2, a0, ALU.add))
            pool.sem_inc(angles_reduced, 1)

            pool.wait_ge(sines_ready, 1)
            chunks_out(pool, 8)
            for a, b, heads, f0 in ((C_W, QM0, 1, 0), (QM0, KM0, HEADS, ROPE // 2), (KM0, VM0, HEADS, ROPE // 2)):
                rotate(pool, own, proj[:, :, a:b].rearrange("p t (h n) -> p t h n", h=heads), heads, f0, rope_tmp,
                       rotated)

            chunks_out(pool, UKV_C)
            q_rows = scr[:, :, 0:HEADS * QW].rearrange("p t (h n) -> p t h n", h=HEADS)
            for a, b in ((0, 1), (1, HEADS)):
                rotate(pool, own, q_rows[:, :, a:b, NOPE:QW], b - a, 0, rope_tmp_q, rotated_q)

            first_waits = {
                0: (weights_used, L_pq.u0),
                4: (split_lo, UNITS - 2),
                5: (weights_used, UNITS - 4),
                7: (split_lo, UNITS),
                8: (weights_used, UNITS - 2),
                10: (weights_used, UNITS),
                14: (turned, n_groups)}
            assert UNITS % RING == 2

            def gather(head, i, parity):
                for v, table in enumerate((expert_u, expert_v)):
                    if v == 0:
                        hold(pool, routed, head + 1, passed)
                    for k in range(TOPK):
                        if v or not isinstance(head, int) or head:
                            hold(pool, rows_used, head * 2 * TOPK + v * TOPK + k - ROWS + 1, passed)
                        elif k in first_waits:
                            semaphore, value = first_waits[k]
                            hold(pool, semaphore, value, passed)
                        pool.indirect_dma_start(
                            out=expert_rows[:, SLOTS[k], :], out_offset=None, in_=table[:, :],
                            in_offset=bass.IndirectOffsetOnAxis(ap=expert_id[parity][:, k:k + 1], axis=0),
                        ).then_inc(rows_landed[k], 16)

            gather(0, 0, 0)
            gather(1, 0, 1)
            with pool.Fori(1, ROUTER_HEADS * T // 2) as i:
                gather(2 * i, i, 0)
                gather(2 * i + 1, i, 1)

        @block.scalar
        def _(act):
            load_gains(act, ((G_ATTN, g_attn), (G_MEM, g_mem), (G_QA, g_q_a), (G_KVA, g_kv_a)))
            act.dma_start(pos_i[:, :], positions.rearrange("(t p) -> t p", p=P)).then_inc(small_landed, 16)
            act.dma_start(freq[:, :], bcast(freqs, P)).then_inc(small_landed, 16)
            act.dma_start(key_rows[:, 0, :], sub_keys1).then_inc(small_landed, 16)
            act.dma_start(key_rows[:, 1, :], sub_keys2).then_inc(small_landed, 16)

            def root_of(at, n):
                job = NORMS.index(at)
                act.wait_ge(means, job + 1)
                act.activation(root[:, at:at + n], mean[:, at:at + n], ACT.Sqrt).then_inc(roots, 1)
                act.wait_ge(rstd_ready, job + 1)

            def squares_of(at, parts):
                for n, (src, junk) in enumerate(parts):
                    ins = act.activation(junk, src, ACT.Square, accum_out=ssq[:, at + n:at + n + 1])
                ins.then_inc(squares, 1)
                root_of(at, len(parts))

            def group_hi(g, j, to, gain):
                act.wait_ge(turned, g + 1)
                src = group_bank(g)
                if gain is None:
                    ins = act.copy(to[0][:, 2 * j:2 * j + 2, :].rearrange("p k n -> p (k n)"), src[:, :])
                else:
                    for k in range(2):
                        ins = act.activation(to[0][:, 2 * j + k, :], src[:, k * SEQ:(k + 1) * SEQ], ACT.Copy,
                                             scale=gains[:, gain + 2 * j + k:gain + 2 * j + k + 1])
                ins.then_inc(turned_hi, 1)

            def turn_hi(name, gain):
                g0, n = TG[name]
                for j in range(n):
                    group_hi(g0 + j, j, xt_a, gain)

            def split(unit, i=0, n=NCH):
                b = unit % RING
                act.wait_ge(weights_landed[b], 16 * (unit // RING + 1 + 4 * i))
                if not isinstance(i, int) or unit + 16 * i >= RING:
                    act.wait_ge(weights_used, unit + 16 * i - RING + 1)
                act.copy(w_parts[0][:, b, :, 0:n], raw[:, b, :, 0:n]).then_inc(split_hi, 1)

            def chunk_out(c, units, dst, n=NCH, norm=None):
                src = bank[2 * (c % 2)][:, 0:n]
                if norm is None:
                    act.wait_ge(weights_used, units)
                    ins = act.copy(dst, src)
                else:
                    hold(act, weights_used, units, passed)
                    ins = act.activation(dst, src, ACT.Copy, scale=rstd[:, norm:norm + 1])
                ins.then_inc(chunk_free[c % 2], 1)

            def pair_out(L, i, dst, last=NCH, norm=None, others={}, beside={}):
                for cc in range(2):
                    for j in range(PER_CHUNK):
                        u = L.u0 + LEAD + PER_CHUNK * cc + j
                        if isinstance(i, int):
                            u += 16 * i
                            whole = last == NCH or not 56 <= u < 64
                            if u < UNITS:
                                split(u, 0, NCH if whole else last)
                        else:
                            split(u, i)
                        for kind, at in beside.get((cc, j), ()):
                            step(kind, at)
                        if (cc, j) in others:
                            others[cc, j]()
                    n = last if cc else NCH
                    chunk_out(L.c0 + cc, L.u0 + 16 * i + PER_CHUNK * (cc + 1), dst(2 * i + cc, n), n, norm)

            def step(kind, j):
                g = STEP_G[kind, j]
                if kind == "x":
                    group_hi(g, j, xt_a, G_ATTN)
                if kind == "h1":
                    group_hi(g, j, xt_b, G_CROSS)
                if kind == "h2":
                    group_hi(g, j, xt_a, G_FFN)
                if kind == "co":
                    group_hi(g, j, xt_b, None)
                if kind in ("k", "q", "rq") and j % 2:
                    act.wait_ge(turned, g + 1)
                    to = {"k": mt, "q": xt32, "rq": xt_pq}[kind]
                    act.copy(to[:, 2 * j:2 * j + 2, :].rearrange("p k n -> p (k n)"),
                             group_bank(g)[:, :]).then_inc(turned_free[g % 4], 1)
                if kind == "s":
                    act.wait_ge(cr_nmx, j + 1)
                    for t in range(T):
                        ins = act.activation(cross_p[:, t * SEQ:(t + 1) * SEQ], group_bank(g)[:, t * SEQ:(t + 1) * SEQ],
                                             ACT.Exp, scale=(D // CROSS_HEADS) ** -0.5,
                                             bias=nmx[:, t:t + 1], accum_out=den[:, t:t + 1])
                    ins.then_inc(turned_free[g % 4], 1)
                if kind == "p":
                    act.wait_ge(turned, g + 1)
                    act.copy(cross_pT, group_bank(g)[:, :]).then_inc(turned_free[g % 4], 1)
                if kind == "rs" and j % 2:
                    act.wait_ge(turned, g + 1)
                    act.copy(scr[:, 1, j // 2 * NCH:(j // 2 + 1) * NCH],
                             group_bank(g)[:, :]).then_inc(turned_free[g % 4], 1)

            def product(L, beside, norm=None, others={}, to=scr):
                for n in range(CHUNKS):
                    u = L.u0 + PER_CHUNK * n
                    for j in range(PER_CHUNK):
                        if u + LEAD + j < UNITS:
                            split(u + LEAD + j)
                        for kind, at in beside.get((n, j), ()):
                            step(kind, at)
                        if (n, j) in others:
                            others[n, j]()
                    if norm is not None:
                        chunk_out(L.c0 + n, u + PER_CHUNK, to[:, 0, n * NCH:(n + 1) * NCH], norm=norm)

            act.wait_ge(turned_free[0], 1)
            step("x", 0)
            for u in range(LEAD):
                step("x", u + 1)
                split(u)

            def proj_cols(c, n):
                return proj[:, 0, bass.ds(c * NCH, n)]

            def load_mem():
                act.dma_start(mem_rows, mem.rearrange("(t p) n -> p t n", p=P)).then_inc(mem_landed, 16)

            def square(rows, at, t):
                if at == N_MEM:
                    act.wait_ge(mem_landed, 16)
                ins = act.activation(scr[:, t, :], rows[:, t, :], ACT.Square, accum_out=ssq[:, at + t:at + t + 1])
                if t == T - 1:
                    ins.then_inc(squares, 1)

            def sines():
                act.wait_ge(angles_ready, 1)
                act.activation(sin[:, :, :], ang[0], ACT.Sin)
                act.activation(cos[:, :, :], ang[1], ACT.Sin).then_inc(sines_ready, 1)

            pair_out(L_in, 0, proj_cols, norm=N_X, beside=BESIDE_IN, others={
                (0, 4): load_mem, (0, 5): lambda: square(h, N_X, 0), (0, 6): lambda: square(h, N_X, 1),
                (0, 7): lambda: root_of(N_X, T),
                (1, 1): lambda: square(mem_rows, N_MEM, 0), (1, 3): lambda: square(mem_rows, N_MEM, 1),
                (1, 4): lambda: root_of(N_MEM, T), (1, 6): sines})
            with act.Fori(1, 3) as i:
                pair_out(L_in, i, proj_cols, norm=N_X)
            pair_out(L_in, 3, proj_cols, LAST_CHUNK_IN, norm=N_X)
            turn_hi("mem", G_MEM)
            chunks_out(act, 8)
            squares_of(N_C, [(proj[:, t, a:b], cross_v[:, t, a:b])
                             for a, b in ((0, Q_RANK), (Q_RANK, C_W)) for t in range(T)])

            def scr_cols(c, n):
                return scr[:, 0, bass.ds(c * NCH, n)]

            with act.Fori(0, PAIRS) as i:
                pair_out(L_ck, i, scr_cols, norm=N_MEM)
            product(L_cv, BESIDE_CV, N_MEM, to=cross_v)
            turn_hi("c", G_QA)
            for n in range(3):
                for k in range(2):
                    split(UQ_U + 2 * n + k + LEAD)
                chunk_out(UQ_C + n, UQ_U + 2 * n + 2, scr[:, 0, n * NCH:(n + 1) * NCH], norm=N_C)
            q_rows = scr[:, :, 0:HEADS * QW]

            def stage(i):
                act.copy(q_stage, q_rows[:, :, bass.ds(i * QW, QW)])
                act.copy(k_stage, kv_up[:, :, bass.ds(i * KVW, NOPE)]).then_inc(staged_a, 1)

            for n in range(4):
                split(UKV_U + n + LEAD)
                if n == 2:
                    act.wait_ge(rotated_q, 1)
                    chunks_out(act, UKV_C + 1)
                    stage(0)
                chunk_out(UKV_C + n, UKV_U + n + 1, kv_up[:, 0, n * NCH:(n + 1) * NCH], norm=N_C + T)

            def turned_out(i):
                act.wait_ge(head_T, 3 * i + 2)
                act.copy(qk_mla, bank[4][:, :])
                act.copy(qr_T, bank[6][0:ROPE, 0:SEQ]).then_inc(head_T_a, 1)

            def head(i, left):
                for m, scale in ((0, QW ** -0.5), (1, HD ** -0.5)):
                    act.wait_ge(head_nmx, 2 * i + m + 1)
                    for t in range(T):
                        a, b = (0, P) if t == 0 else (P, S3)
                        ins = act.activation(pr[m][:, a:b], sc[m][:, a:b], ACT.Exp, scale=scale,
                                             bias=nmx[:, 2 * m + t:2 * m + t + 1],
                                             accum_out=den[:, 2 * m + t:2 * m + t + 1])
                    ins.then_inc(head_P, 1)
                if left > 0:
                    turned_out(i + 1)
                if left > 1:
                    stage(i + 2)
                act.wait_ge(head_PT, 2 * i + 1)
                act.copy(prT[0], bank[0][:, 0:S3]).then_inc(head_PT_a, 1)
                act.wait_ge(head_rden, 2 * i + 1)
                hold(act, head_O, 2 * i + 1, passed)
                for t in range(T):
                    ins = act.activation(kv_up[:, t, bass.ds(i * KVW, NOPE)], bank[2][:, t * P:(t + 1) * P],
                                         ACT.Copy, scale=rden[:, t:t + 1])
                ins.then_inc(head_O_a, 1)

            turned_out(0)
            chunks_out(act, L_out.c0)
            act.wait_ge(rotated_q, 2)
            stage(1)
            head(0, HEADS - 1)
            with act.Fori(1, HEADS - 2) as i:
                head(i, 2)
            head(HEADS - 2, 1)
            head(HEADS - 1, 0)

            act.wait_ge(head_O_a, HEADS)
            act.wait_ge(head_O_v, HEADS)
            turn_hi("mix", G_MIX)

            def residual_norm(at, count):
                def square(t):
                    act.wait_ge(residual, count)
                    ins = act.activation(scr[:, t, :], h[:, t, :], ACT.Square, accum_out=ssq[:, at + t:at + t + 1])
                    if t == T - 1:
                        ins.then_inc(squares, 1)

                return {(0, 5): lambda: square(0), (0, 6): lambda: square(1), (0, 7): lambda: root_of(at, T)}

            def stage_first():
                group_out(act, STEP_G["rs", 0])
                act.copy(half_s.rearrange("p k n -> p (k n)"), scr[:, 0, 0:2 * NKEYS]).then_inc(half_staged, 1)

            def mix_square(n, t):
                at = N_MIX + n * T + t
                ins = act.activation(mix_half(t, n), mixed[t][n], ACT.Square, accum_out=ssq[:, at:at + 1])
                if (n, t) == (1, T - 1):
                    ins.then_inc(squares, 1)
                    root_of(N_MIX, 2 * T)

            product(L_out, BESIDE_OUT, others={(0, 0): lambda: mix_square(0, 0), (0, 1): lambda: mix_square(0, 1),
                                               (0, 2): lambda: mix_square(1, 0), (0, 3): lambda: mix_square(1, 1)})
            product(L_cq, BESIDE_CQ, N_H1, residual_norm(N_H1, 1))
            for kind, j in AFTER_CQ:
                step(kind, j)
            product(L_co, BESIDE_CO)
            product(L_pq, BESIDE_PQ, N_H2, {**residual_norm(N_H2, 2), (1, 6): stage_first})
            for kind, j in AFTER_PQ:
                step(kind, j)

            heads = ROUTER_HEADS * T
            scores = scr[:, :, :].rearrange("p t n -> p (t n)")

            def stage(head):
                hold(act, half_used, head, passed)
                act.copy(half_s.rearrange("p k n -> p (k n)"),
                         scores[:, bass.ds(head * 2 * NKEYS, 2 * NKEYS)]).then_inc(half_staged, 1)

            def gates(head, parity):
                act.wait_ge(routed, head + 1)
                act.activation(gate[parity][:, :], best, ACT.Exp, bias=neg_best[parity][:, 0:1],
                               accum_out=gate_sum[parity][:, 0:1]).then_inc(gates_ready, 1)

            def gelu(head):
                act.wait_ge(rows_used, head * 2 * TOPK + TOPK)
                act.activation(act_out, act_in, ACT.Gelu).then_inc(activated, 1)

            gates(0, 0)
            groups_out(act, n_groups)
            stage(1)

            def head_pairs(a, b):
                with act.Fori(a, b) as i:
                    for parity in range(2):
                        head_no = 2 * i + parity
                        gelu(head_no)
                        gates(head_no + 1, 1 - parity)
                        stage(head_no + 2)

            head_pairs(0, heads // 4)
            act.wait_ge(residual, 3)
            squares_of(N_OUT, [(h[:, 0, :], scr[:, 0, :])])
            head_pairs(heads // 4, heads // 2 - 1)
            gelu(heads - 2)
            gates(heads - 1, 1)
            gelu(heads - 1)
            act.activation(root[:, N_OUT:N_OUT + 1], mean[:, N_OUT:N_OUT + 1], ACT.Sqrt)
            act.wait_ge(residual, 4)
            squares_of(N_OUT + 1, [(h[:, 1, 0:D // 2], scr[:, 1, 0:D // 2])])

        @block.vector
        def _(dve):
            own = Own(dve, vec)

            def norm_of(at, widths):
                job, first = NORMS.index(at), at
                dve.wait_ge(squares, job + 1)
                for n, w in widths:
                    ins = dve.tensor_scalar(mean[:, at:at + n], ssq[:, at:at + n], 1.0 / w, EPS, ALU.mult, ALU.add)
                    at += n
                ins.then_inc(means, 1)
                dve.wait_ge(roots, job + 1)
                dve.reciprocal(rstd[:, first:at], root[:, first:at]).then_inc(rstd_ready, 1)
                dve.wait_ge(rstd_ready, job + 1)

            hi_groups = [0]

            def group_lo(g, j, to, gain):
                hi_groups[0] += 1
                dve.wait_ge(turned_hi, hi_groups[0])
                src = group_bank(g)
                hi, lo = to
                for k in range(2):
                    if gain is None:
                        ins = dve.tensor_tensor(lo[:, 2 * j + k, :], src[:, k * SEQ:(k + 1) * SEQ],
                                                hi[:, 2 * j + k, :].bitcast(F32), ALU.subtract)
                    else:
                        ins = dve.scalar_tensor_tensor(
                            out=lo[:, 2 * j + k, :], in0=src[:, k * SEQ:(k + 1) * SEQ],
                            scalar=gains[:, gain + 2 * j + k:gain + 2 * j + k + 1],
                            in1=hi[:, 2 * j + k, :].bitcast(F32), op0=ALU.mult, op1=ALU.subtract)
                ins.then_inc(turned_free[g % 4], 1)

            def turn_lo(name, gain):
                g0, n = TG[name]
                for j in range(n):
                    group_lo(g0 + j, j, xt_a, gain)

            def split(unit, i=0, n=NCH):
                b = unit % RING
                dve.wait_ge(split_hi, unit + 16 * i + 1)
                dve.tensor_tensor(w_parts[1][:, b, :, 0:n], raw[:, b, :, 0:n],
                                  w_parts[0][:, b, :, 0:n].bitcast(F32), ALU.subtract).then_inc(split_lo, 1)

            def chunk_out(c, units, dst, norm, n=NCH):
                dve.wait_ge(weights_used, units)
                dve.tensor_scalar(dst, bank[2 * (c % 2) + 1][:, 0:n], rstd[:, norm + 1:norm + 2], None,
                                  ALU.mult).then_inc(chunk_free[c % 2], 1)

            def chunk_add(c, units, col, norm=None):
                dve.wait_ge(weights_used, units)
                for t in range(T):
                    to, src = h[:, t, bass.ds(col, NCH)], bank[2 * (c % 2) + t][:, :]
                    if norm is None:
                        ins = dve.tensor_tensor(to, to, src, ALU.add)
                    else:
                        ins = dve.scalar_tensor_tensor(out=to, in0=src, scalar=rstd[:, norm + t:norm + t + 1],
                                                       in1=to, op0=ALU.mult, op1=ALU.add)
                    ins.then_inc(chunk_free[c % 2], 1)

            def pair_out(L, i, dst, last=NCH, norm=None, others={}, beside={}):
                for cc in range(2):
                    for j in range(PER_CHUNK):
                        u = L.u0 + LEAD + PER_CHUNK * cc + j
                        if isinstance(i, int):
                            u += 16 * i
                            whole = last == NCH or not 56 <= u < 64
                            if u < UNITS:
                                split(u, 0, NCH if whole else last)
                        else:
                            split(u, i)
                        for kind, at in beside.get((cc, j), ()):
                            step(kind, at)
                        if (cc, j) in others:
                            others[cc, j]()
                    n = last if cc else NCH
                    chunk_out(L.c0 + cc, L.u0 + 16 * i + PER_CHUNK * (cc + 1), dst(2 * i + cc, n), norm, n)

            def step(kind, j):
                g = STEP_G[kind, j]
                if kind == "x":
                    group_lo(g, j, xt_a, G_ATTN)
                if kind == "consts":
                    dve.wait_ge(turned, g + 1)
                    dve.tensor_copy(pos_t[:, :], group_bank(g)[:, 0:T])
                    own.link(dve.tensor_copy(keys_T[:, :, :],
                                             group_bank(g)[:, P:3 * P].rearrange("p (k n) -> p k n", k=2)))
                    dve.sem_inc(turned_free[g % 4], 1)
                if kind == "h1":
                    group_lo(g, j, xt_b, G_CROSS)
                if kind == "h2":
                    group_lo(g, j, xt_a, G_FFN)
                if kind == "co":
                    group_lo(g, j, xt_b, None)
                if kind in ("k", "q", "rq") and j % 2 == 0:
                    dve.wait_ge(turned, g + 1)
                    to = {"k": mt, "q": xt32, "rq": xt_pq}[kind]
                    dve.tensor_copy(to[:, 2 * j:2 * j + 2, :].rearrange("p k n -> p (k n)"),
                                    group_bank(g)[:, :]).then_inc(turned_free[g % 4], 1)
                if kind == "s":
                    dve.wait_ge(turned, g + 1)
                    own.link(dve.tensor_reduce(mx[:, 0:T], tiled(group_bank(g)[:, :]), AX, ALU.max))
                    dve.tensor_scalar(nmx[:, 0:T], mx[:, 0:T], -(D // CROSS_HEADS) ** -0.5, None,
                                      ALU.mult).then_inc(cr_nmx, 1)
                if kind == "p":
                    group_out(dve, STEP_G["s", j])
                    for t in range(T if j else 0):
                        group_out(dve, STEP_G["o", T * (j - 1) + t])
                    own.link(dve.reciprocal(rden[:, 0:T], den[:, 0:T]))
                if kind == "o":
                    dve.wait_ge(turned, g + 1)
                    hd, t = j // T, j % T
                    dve.tensor_scalar(scr[:, t, hd * NCH:(hd + 1) * NCH], group_bank(g)[:, :], rden[:, t:t + 1], None,
                                      ALU.mult).then_inc(turned_free[g % 4], 1)
                if kind == "rs" and j % 2 == 0:
                    dve.wait_ge(turned, g + 1)
                    dve.tensor_copy(scr[:, 0, j // 2 * NCH:(j // 2 + 1) * NCH],
                                    group_bank(g)[:, :]).then_inc(turned_free[g % 4], 1)

            def product(L, beside, norm=None, add=None, others={}, to=scr):
                for n in range(CHUNKS):
                    u = L.u0 + PER_CHUNK * n
                    parts = len(add) if add else 1
                    for j in range(PER_CHUNK):
                        if u + LEAD + j < UNITS:
                            split(u + LEAD + j)
                        for kind, at in beside.get((n, j), ()):
                            step(kind, at)
                        if (n, j) in others:
                            others[n, j]()
                        part, end = divmod(j + 1, PER_CHUNK // parts)
                        if add and end == 0:
                            chunk_add(L.c0 + parts * n + part - 1, u + j + 1, n * NCH, add[part - 1])
                    if not add:
                        chunk_out(L.c0 + n, u + PER_CHUNK, to[:, 1, n * NCH:(n + 1) * NCH], norm)

            dve.wait_ge(turned, 1)
            own.link(dve.tensor_copy(gains[:, :], bank[4][:, 0:G_ROWS]))
            dve.sem_inc(turned_free[0], 1)
            step("x", 0)
            for u in range(LEAD):
                step("x", u + 1)
                split(u)
            dve.wait_ge(small_landed, 16 * 4)
            dve.tensor_copy(pos_f[:, :], pos_i[:, :]).then_inc(pos_ready, 1)

            def proj_cols(c, n):
                return proj[:, 1, bass.ds(c * NCH, n)]

            def arguments():
                dve.wait_ge(angles_reduced, 1)
                a0, a1 = ang[0], ang[1]
                own.link(dve.tensor_scalar(a0, a0, 3.1415925, -3.1415925, ALU.min, ALU.max))
                own.link(dve.scalar_tensor_tensor(out=a1, in0=a0, scalar=-1.0, in1=a0, op0=ALU.mult, op1=ALU.max))
                dve.tensor_scalar(a1, a1, -1.0, math.pi / 2, ALU.mult, ALU.add).then_inc(angles_ready, 1)

            pair_out(L_in, 0, proj_cols, norm=N_X, beside=BESIDE_IN, others={
                (0, 7): lambda: norm_of(N_X, [(T, D)]), (1, 4): lambda: norm_of(N_MEM, [(T, D)]),
                (1, 5): arguments})
            with dve.Fori(1, 3) as i:
                pair_out(L_in, i, proj_cols, norm=N_X)
            pair_out(L_in, 3, proj_cols, LAST_CHUNK_IN, norm=N_X)
            turn_lo("mem", G_MEM)
            norm_of(N_C, [(T, Q_RANK), (T, KV_RANK)])
            with dve.Fori(0, PAIRS) as i:
                pair_out(L_ck, i, lambda c, n: scr[:, 1, bass.ds(c * NCH, n)], norm=N_MEM)
            product(L_cv, BESIDE_CV, N_MEM, to=cross_v)
            turn_lo("c", G_QA)
            g = TG["kr"][0]
            dve.wait_ge(turned, g + 1)
            dve.tensor_copy(kr_T[:, :], group_bank(g)[0:ROPE, 0:SEQ]).then_inc(turned_free[g % 4], 1)
            for n in range(3):
                for k in range(2):
                    split(UQ_U + 2 * n + k + LEAD)
                chunk_out(UQ_C + n, UQ_U + 2 * n + 2, scr[:, 1, n * NCH:(n + 1) * NCH], N_C)
            def stage(i):
                dve.tensor_copy(qm_stage, proj[:, :, bass.ds(i * HD + QM0, HD)])
                dve.tensor_copy(km_stage, proj[:, :, bass.ds(i * HD + KM0, HD)]).then_inc(staged_v, 1)

            for n in range(4):
                split(UKV_U + n + LEAD)
                if n == 2:
                    dve.wait_ge(rotated, 3)
                    stage(0)
                chunk_out(UKV_C + n, UKV_U + n + 1, kv_up[:, 1, n * NCH:(n + 1) * NCH], N_C + T)
            chunks_out(dve, L_out.c0)

            HEAD_STEPS = 6

            def turned_out(i):
                dve.wait_ge(head_T, 3 * i + 3)
                dve.tensor_copy(qk_moba, bank[5][:, :]).then_inc(head_T_v, 1)

            def maxima(i):
                step = Own(dve, vec_heads, HEAD_STEPS * i)
                for m, scale in ((0, QW ** -0.5), (1, HD ** -0.5)):
                    dve.wait_ge(head_S, 2 * i + m + 1)
                    step.link(dve.tensor_tensor(sc[m], bank[7 if m else 3][:, 0:S3], mask[:, :], ALU.add))
                    for t in range(T):
                        a, b = (0, P) if t == 0 else (P, S3)
                        step.mark(dve.tensor_reduce(mx[:, 2 * m + t:2 * m + t + 1], sc[m][:, a:b], AX, ALU.max))
                    step.wait()
                    dve.tensor_scalar(nmx[:, 2 * m:2 * m + 2], mx[:, 2 * m:2 * m + 2], -scale, None,
                                      ALU.mult).then_inc(head_nmx, 1)
                assert step.n == HEAD_STEPS

            def head(i, left):
                if not isinstance(i, int) or i:
                    dve.wait_ge(head_O_v, i)
                for m in range(2):
                    dve.wait_ge(head_P, 2 * i + m + 1)
                    dve.reciprocal(rden[:, 2 * m:2 * m + 2], den[:, 2 * m:2 * m + 2]).then_inc(head_rden, 1)
                if left > 0:
                    turned_out(i + 1)
                if left > 1:
                    stage(i + 2)
                dve.wait_ge(head_PT, 2 * i + 2)
                dve.tensor_copy(prT[1], bank[1][:, 0:S3]).then_inc(head_PT_v, 1)
                if left > 0:
                    maxima(i + 1)
                dve.wait_ge(head_rden, 2 * i + 2)
                dve.wait_ge(head_O, 2 * i + 2)
                for t in range(T):
                    ins = dve.tensor_scalar(proj[:, t, bass.ds(i * HD + QM0, HD)], bank[1][:, t * P:(t + 1) * P],
                                            rden[:, 2 + t:3 + t], None, ALU.mult)
                ins.then_inc(head_O_v, 1)

            dve.wait_ge(made_consts, 3)
            turned_out(0)
            stage(1)
            maxima(0)
            head(0, HEADS - 1)
            with dve.Fori(1, HEADS - 2) as i:
                head(i, 2)
            head(HEADS - 2, 1)
            head(HEADS - 1, 0)
            turn_lo("mix", G_MIX)

            def residual_done(c):
                chunks_out(dve, c)
                dve.sem_inc(residual, 1)

            product(L_out, BESIDE_OUT, add=[N_MIX, N_MIX + T],
                    others={(0, 3): lambda: norm_of(N_MIX, [(2 * T, HEADS * HD)])})
            residual_done(L_cq.c0)
            product(L_cq, BESIDE_CQ, norm=N_H1, others={(0, 7): lambda: norm_of(N_H1, [(T, D)])})
            for kind, j in AFTER_CQ:
                step(kind, j)
            product(L_co, BESIDE_CO, add=[None])
            residual_done(L_pq.c0)

            heads = ROUTER_HEADS * T
            r = Own(dve, vec_route)

            def top16(r, values, left, tops, places):
                r.link(dve.max(tops[:, 0:8], values))
                r.mark(dve.match_replace(left, tops[:, 0:8], values, LEAST))
                r.mark(dve.max_index(places[:, 0:8], tops[:, 0:8], values))
                r.wait()
                r.link(dve.max(tops[:, 8:16], left))
                r.link(dve.max_index(places[:, 8:16], tops[:, 8:16], left))

            def route_half(head, s):
                if s == 0:
                    dve.sem_clear(vec_route)
                    hold(dve, half_staged, head + 1, passed)
                    r.n = 0
                top16(r, half_s[:, s, :], half_left[:, s, :], top_v[:, s, :], top_i[:, s, :])
                if s == 1:
                    dve.sem_inc(half_used, 1)

            def route_cands(head):
                r.mark(dve.tensor_copy(top_f[:, :, :], top_i[:, :, :]))
                r.mark(dve.tensor_tensor(cand.rearrange("p (a b) -> p a b", a=TOPK),
                                         top_v[:, 0, :].unsqueeze(2).to_broadcast((P, TOPK, TOPK)),
                                         top_v[:, 1, :].unsqueeze(1).to_broadcast((P, TOPK, TOPK)), ALU.add))
                r.wait()

            def route_best(head):
                if not isinstance(head, int) or head:
                    hold(dve, gates_ready, head, passed)
                top16(r, cand, cand_left, best, spot)
                r.mark(dve.tensor_scalar(spot_ab[:, 0, :], spot, 4, None, ALU.logical_shift_right))
                r.mark(dve.tensor_scalar(spot_ab[:, 1, :], spot, TOPK - 1, None, ALU.bitwise_and))
                r.wait()
                r.link(dve.tensor_copy(spot_f[:, :, :], spot_ab[:, :, :]))

            def route_ids(head, parity):
                for s in range(2):
                    r.mark(dve.tensor_tensor(hot[s], spot_f[:, s, :].unsqueeze(2).to_broadcast((P, TOPK, TOPK)),
                                             counts[:, :].unsqueeze(1).to_broadcast((P, TOPK, TOPK)), ALU.is_equal))
                r.wait()
                for s in range(2):
                    r.mark(dve.tensor_tensor(hot[s], hot[s],
                                             top_f[:, s, :].unsqueeze(1).to_broadcast((P, TOPK, TOPK)), ALU.mult))
                r.wait()
                for s in range(2):
                    r.mark(dve.tensor_reduce(chosen[:, s, :], hot[s], AX, ALU.add))
                r.wait()
                if not isinstance(head, int) or head >= 2:
                    dve.wait_ge(rows_used, (head - 1) * 2 * TOPK)
                r.mark(dve.tensor_scalar(neg_best[parity][:, :], best[:, 0:1], -1.0, None, ALU.mult))
                r.link(dve.scalar_tensor_tensor(out=expert_id[parity][:, :], in0=chosen[:, 0, :], scalar=float(NKEYS),
                                                in1=chosen[:, 1, :], op0=ALU.mult, op1=ALU.add))
                dve.sem_inc(routed, 1)

            def route(head, parity):
                route_half(head, 0)
                route_half(head, 1)
                route_cands(head)
                route_best(head)
                route_ids(head, parity)

            def token_rows(t):
                own.mark(dve.scalar_tensor_tensor(out=mt_rows[:, t, :], in0=h[:, t, :],
                                                  scalar=rstd[:, N_H2 + t:N_H2 + t + 1],
                                                  in1=gain_wide, op0=ALU.mult, op1=ALU.mult))

            dve.wait_ge(made_consts, 3)
            dve.wait_ge(gain_landed, 16)
            product(L_pq, BESIDE_PQ, norm=N_H2, others={
                (0, 7): lambda: norm_of(N_H2, [(T, D)]), (1, 0): lambda: token_rows(0), (1, 6): lambda: token_rows(1),
                (1, 7): lambda: (own.wait(), route_half(0, 0)), (2, 0): lambda: route_half(0, 1),
                (2, 1): lambda: route_cands(0), (2, 2): lambda: route_best(0), (2, 3): lambda: route_ids(0, 0)})
            for kind, j in AFTER_PQ:
                step(kind, j)

            def dots(head, t):
                for k in range(TOPK):
                    dve.wait_ge(rows_landed[k], 32 * head + 16)
                    dve.tensor_tensor_reduce(expert_rows[:, SLOTS[k], :], expert_rows[:, SLOTS[k], :], mt_rows[:, t, :], 1.0, 0.0,
                                             ALU.mult, ALU.add, act_in[:, k:k + 1]).then_inc(rows_used, 1)

            def combine(head, t, parity):
                dve.sem_clear(vec_route)
                r = Own(dve, vec_route)
                dve.wait_ge(gates_ready, head + 1)
                r.link(dve.reciprocal(gate_inv[parity][:, :], gate_sum[parity][:, :]))
                dve.wait_ge(activated, head + 1)
                r.link(dve.scalar_tensor_tensor(out=weight, in0=act_out, scalar=gate_inv[parity][:, 0:1],
                                                in1=gate[parity][:, :], op0=ALU.mult, op1=ALU.mult))
                for k in range(TOPK):
                    dve.wait_ge(rows_landed[k], 32 * head + 32)
                    dve.wait_ge(rows_used, head * 2 * TOPK + TOPK + k)
                    dve.scalar_tensor_tensor(out=h[:, t, :], in0=expert_rows[:, SLOTS[k], :], scalar=weight[:, k:k + 1],
                                             in1=h[:, t, :], op0=ALU.mult, op1=ALU.add).then_inc(rows_used, 1)

            for t in range(T):
                first = ROUTER_HEADS * t
                stop = ROUTER_HEADS // 2 - (t == T - 1)

                def pair(i, last=False):
                    for parity in range(2):
                        head_no = first + 2 * i + parity
                        dots(head_no, t)
                        if not (last and parity):
                            route(head_no + 1, 1 - parity)
                        combine(head_no, t, parity)

                if t == 0:
                    pair(0)
                with dve.Fori(1 if t == 0 else 0, stop) as i:
                    pair(i)
                if t == T - 1:
                    pair(stop, True)
                dve.wait_ge(rows_used, heads // T * (t + 1) * 2 * TOPK)
                dve.sem_inc(residual, 1)
                if t == T - 1:
                    own.link(dve.tensor_tensor_reduce(scr[:, 1, D // 2:D], h[:, t, D // 2:D], h[:, t, D // 2:D], 1.0, 0.0,
                                                      ALU.mult, ALU.add, ssq[:, N_COLS - 1:N_COLS]))
                    dve.wait_ge(squares, NORMS.index(N_OUT + t) + 1)
                    own.link(dve.tensor_tensor(ssq[:, N_OUT + t:N_OUT + t + 1], ssq[:, N_OUT + t:N_OUT + t + 1],
                                               ssq[:, N_COLS - 1:N_COLS], ALU.add))
                norm_of(N_OUT + t, [(1, D)])
                dve.wait_ge(gain_landed, 32)
                for a in range(0, D, D // 2):
                    dve.scalar_tensor_tensor(out=mt_rows[:, t, a:a + D // 2], in0=h[:, t, a:a + D // 2],
                                             scalar=rstd[:, N_OUT + t:N_OUT + t + 1], in1=final_gain[:, a:a + D // 2],
                                             op0=ALU.mult, op1=ALU.mult).then_inc(normed, 1)
        @block.tensor
        def _(pe):
            def turn(name, rows):
                g0, n = TG[name]
                for j in range(n):
                    g = g0 + j
                    if g >= 4:
                        pe.wait_ge(turned_free[g % 4], g // 4)
                    for k in range(2):
                        for t in range(T):
                            ins = pe.transpose(group_bank(g)[:, (2 * k + t) * P:(2 * k + t + 1) * P],
                                               rows(t, 2 * j + k), ident[:, :])
                    ins.then_inc(turned, 1)

            def chunk(c, units, i=0, n=NCH, free=None, kb0=0, ahead=None, operand=xt_a,
                      groups=None):
                if free is not None:
                    pe.wait_ge(chunk_free[c % 2], free)
                for at, u in enumerate(units):
                    if ahead and at in ahead:
                        ahead[at]()
                    if groups:
                        group_out(pe, groups(at))
                    pe.wait_ge(split_lo, u + 16 * i + 1)
                    w = [part[:, u % RING, :, 0:n] for part in w_parts]
                    for k in range(UB):
                        for t in range(T):
                            kb = kb0 + at * UB + k
                            to = bank[2 * (c % 2) + t][:, 0:n]
                            x_hi, x_lo = (part[:, kb, t * P:(t + 1) * P] for part in operand)
                            pe.matmul(to, x_hi, w[0][:, k, :], start=(at + k == 0), stop=False)
                            pe.matmul(to, x_hi, w[1][:, k, :], start=False, stop=False)
                            ins = pe.matmul(to, x_lo, w[0][:, k, :], start=False,
                                            stop=(at == len(units) - 1 and k == UB - 1))
                    ins.then_inc(weights_used, 1)

            def pair(L, i, last=NCH, first=False, ahead=None, groups=None):
                for cc in range(2):
                    c, u = L.c0 + cc, L.u0 + PER_CHUNK * cc
                    chunk(c, range(u, u + PER_CHUNK), i, last if cc else NCH,
                          None if first else 2 * uses(c, c % 2) + 2 * i, ahead=None if cc else ahead,
                          groups=None if cc else groups)

            def step(kind, j):
                g = STEP_G[kind, j]
                if g >= 4:
                    group_out(pe, g - 4)
                to = group_bank(g)
                rows = scr
                if kind == "x":
                    pe.wait_ge(x_landed[j // 2], 16)
                    rows = h
                if kind == "consts":
                    pe.wait_ge(small_landed, 16 * 4)
                    pe.wait_ge(pos_ready, 1)
                    pe.transpose(to[:, 0:T], pos_f[:, :], ident[0:T, 0:T])
                    pe.transpose(to[:, P:2 * P], key_rows[:, 0, :], ident[:, :])
                    ins = pe.transpose(to[:, 2 * P:3 * P], key_rows[:, 1, :], ident[:, :])
                if kind == "h1":
                    columns_out(pe, L_out, j // 2, 2)
                    rows = h
                if kind == "h2":
                    columns_out(pe, L_co, j // 2)
                    rows = h
                if kind == "k":
                    columns_out(pe, L_ck, j // 2)
                    pe.wait_ge(rotated, 3)
                if kind == "q":
                    columns_out(pe, L_cq, j // 2)
                if kind == "rq":
                    columns_out(pe, L_pq, j // 2)
                if kind == "co":
                    for t in range(T):
                        group_out(pe, STEP_G["o", j // 2 * T + t])
                if kind in ("x", "k", "h1", "h2", "q", "rq", "co"):
                    for k in range(2):
                        for t in range(T):
                            kb = 2 * j + k
                            ins = pe.transpose(to[:, (2 * k + t) * P:(2 * k + t + 1) * P],
                                               rows[:, t, kb * P:(kb + 1) * P], ident[:, :])
                if kind == "s":
                    for q in range(CB // 2):
                        group_out(pe, STEP_G["q", j * CB // 2 + q])
                    for t in range(T):
                        for k in range(CB):
                            ins = pe.matmul(to[:, t * SEQ:(t + 1) * SEQ], xt32[:, CB * j + k, t * P:(t + 1) * P],
                                            mt[:, CB * j + k, :], start=(k == 0), stop=(k == CB - 1))
                if kind == "p":
                    group_out(pe, STEP_G["s", j])
                    for n in range(T * SEQ // P):
                        ins = pe.transpose(to[:, n * P:(n + 1) * P], cross_p[:, n * P:(n + 1) * P], ident[:, :])
                if kind == "o":
                    hd, t = j // T, j % T
                    group_out(pe, STEP_G["p", hd])
                    for m in range(SEQ // P):
                        at = t * SEQ + m * P
                        ins = pe.matmul(to[:, :], cross_pT[:, at:at + P], cross_v[:, m, hd * NCH:(hd + 1) * NCH],
                                        start=(m == 0), stop=(m == SEQ // P - 1))
                if kind == "rs":
                    n, t = j // T, j % T
                    for q in range(2):
                        group_out(pe, STEP_G["rq", 2 * n + q])
                    for k in range(4):
                        ins = pe.matmul(to[:, k * P:(k + 1) * P], xt_pq[:, 4 * n + k, t * P:(t + 1) * P],
                                        keys_T[:, k % 2, :], start=True, stop=True)
                ins.then_inc(turned, 1)

            def product(L, beside, operand, group, parts=1):
                units = PER_CHUNK // parts
                for n in range(CHUNKS):
                    for part in range(parts):
                        c, u, j0 = L.c0 + parts * n + part, L.u0 + PER_CHUNK * n + units * part, units * part

                        def ahead(j):
                            for kind, at in beside.get((n, j), ()):
                                step(kind, at)

                        chunk(c, range(u, u + units), free=2 * uses(c, c % 2), kb0=UB * j0, operand=operand,
                              ahead={j: lambda j=j: ahead(j0 + j) for j in range(units)},
                              groups=None if n or group is None else lambda j: group(j0 + j))

            pe.wait_ge(made_ident, 1)
            pe.wait_ge(gains_landed, 16 * 8)
            pe.transpose(bank[4][:, 0:G_ROWS], gain_rows[:, :], ident[0:G_ROWS, 0:G_ROWS]).then_inc(turned, 1)
            for kind, j in BEFORE_IN:
                step(kind, j)
            pair(L_in, 0, first=True, groups=lambda j: TG["x"][0] + j,
                 ahead={j: lambda steps=steps: [step(*it) for it in steps] for (_, j), steps in BESIDE_IN.items()})
            with pe.Fori(1, 3) as i:
                pair(L_in, i)
            pair(L_in, 3, LAST_CHUNK_IN)
            pe.wait_ge(mem_landed, 16)
            turn("mem", lambda t, kb: mem_rows[:, t, kb * P:(kb + 1) * P])
            product(L_ck, {}, xt_a, lambda j: TG["mem"][0] + j)
            product(L_cv, BESIDE_CV, xt_a, None)
            turn("c", lambda t, kb: proj[:, t, kb * P:(kb + 1) * P])
            g = TG["kr"][0]
            pe.wait_ge(turned_free[g % 4], g // 4)
            for t in range(T):
                ins = pe.transpose(group_bank(g)[0:ROPE, t * P:(t + 1) * P], proj[:, t, C_W:QM0], ident[:, :])
            ins.then_inc(turned, 1)
            for n in range(3):
                c, u = UQ_C + n, UQ_U + 2 * n
                chunk(c, range(u, u + 2), free=2 * uses(c, c % 2), groups=lambda j: TG["c"][0] + j)
            def head_turns(i):
                for m, (staged, out, q, k) in enumerate(((staged_a, head_T_a, q_stage, k_stage),
                                                         (staged_v, head_T_v, qm_stage, km_stage))):
                    pe.wait_ge(staged, i + 1)
                    if not isinstance(i, int) or i:
                        pe.wait_ge(out, i)
                    for n, rows in enumerate((q, k)):
                        for t in range(T):
                            ins = pe.transpose(bank[4 + m][:, (2 * n + t) * P:(2 * n + t + 1) * P],
                                               rows[:, t, 0:P], ident[:, :])
                    ins.then_inc(head_T, 1)
                    if m == 0:
                        for t in range(T):
                            ins = pe.transpose(bank[6][0:ROPE, t * P:(t + 1) * P], q[:, t, P:QW], ident[:, :])
                        ins.then_inc(head_T, 1)

            for n in range(4):
                c, u = UKV_C + n, UKV_U + n
                if n == 3:
                    groups_out(pe, TG["mix"][0])
                    head_turns(0)
                chunk(c, range(u, u + 1), free=2 * uses(c, c % 2), kb0=Q_RANK // P,
                      groups=lambda j: TG["c"][0] + Q_RANK // P // 2)

            chunks_out(pe, L_out.c0)

            def head_scores(i):
                for m, (qk, b, ready) in enumerate(((qk_mla, 3, head_T_a), (qk_moba, 7, head_T_v))):
                    pe.wait_ge(ready, i + 1)
                    if not isinstance(i, int) or i:
                        pe.wait_ge(head_nmx, 2 * i)
                    for t in range(T):
                        to = bank[b][:, 0:P] if t == 0 else bank[b][:, P:S3]
                        ins = pe.matmul(to, qk[:, t * P:(t + 1) * P], qk[:, SEQ:SEQ + (t + 1) * P],
                                        start=True, stop=(m == 1))
                        if m == 0:
                            ins = pe.matmul(to, qr_T[:, t * P:(t + 1) * P], kr_T[:, 0:(t + 1) * P],
                                            start=False, stop=True)
                    ins.then_inc(head_S, 1)

            def head(i, last=False):
                if not last:
                    head_turns(i + 1)
                for m, free in enumerate((head_PT_a, head_PT_v)):
                    pe.wait_ge(head_P, 2 * i + m + 1)
                    if not isinstance(i, int) or i:
                        pe.wait_ge(free, i)
                        if m:
                            pe.wait_ge(head_O_v, i)
                    for n in range(3):
                        ins = pe.transpose(bank[m][:, n * P:(n + 1) * P], pr[m][:, n * P:(n + 1) * P], ident[:, :])
                    ins.then_inc(head_PT, 1)
                if not last:
                    head_scores(i + 1)
                if not isinstance(i, int) or i:
                    pe.wait_ge(head_O_a, i)
                for m, ready in enumerate((head_PT_a, head_PT_v)):
                    pe.wait_ge(ready, i + 1)
                    v = [kv_up[:, t, bass.ds(i * KVW + NOPE, NOPE)] if m == 0 else
                         proj[:, t, bass.ds(i * HD + VM0, HD)] for t in range(T)]
                    o_bank = bank[2 - m]
                    pe.matmul(o_bank[:, 0:P], prT[m][:, 0:P], v[0], start=True, stop=True)
                    pe.matmul(o_bank[:, P:SEQ], prT[m][:, P:2 * P], v[0], start=True, stop=False)
                    pe.matmul(o_bank[:, P:SEQ], prT[m][:, 2 * P:S3], v[1], start=False, stop=True).then_inc(head_O, 1)

            head_scores(0)
            head(0)
            with pe.Fori(1, HEADS - 1) as i:
                head(i)
            head(HEADS - 1, True)
            pe.wait_ge(head_O_a, HEADS)
            pe.wait_ge(head_O_v, HEADS)
            turn("mix", lambda t, kb: mla_o[:, t, kb, :] if kb < HEADS else
                 moba_o[:, t, (kb - HEADS) * P:(kb - HEADS + 1) * P])

            product(L_out, BESIDE_OUT, xt_a, lambda j: TG["mix"][0] + j, parts=2)
            product(L_cq, BESIDE_CQ, xt_b, lambda j: STEP_G["h1", j])
            for kind, j in AFTER_CQ:
                step(kind, j)
            product(L_co, BESIDE_CO, xt_b, lambda j: STEP_G["co", j])
            product(L_pq, BESIDE_PQ, xt_a, lambda j: STEP_G["h2", j])
            for kind, j in AFTER_PQ:
                step(kind, j)


_NAMES = ['x', 'mem', 'positions', 'freqs', 'g_attn', 'w_in', 'g_q_a', 'w_uq', 'g_kv_a', 'w_ukv', 'g_mla_o',
          'g_moba_o', 'w_out', 'g_cross', 'g_mem', 'w_cq', 'w_ck', 'w_cv', 'w_co', 'g_ffn', 'w_pq', 'sub_keys1',
          'sub_keys2', 'expert_u', 'expert_v', 'g_final']


def kernel(**inputs):
    import numpy as _np
    import concourse.bacc as _bacc
    from concourse import mybir as _mybir
    from concourse.bass_utils import run_bass_kernel_spmd as _run

    nc = _bacc.Bacc("TRN2", target_bir_lowering=False, num_devices=1)
    freqs = _np.concatenate([
        _np.exp(_np.arange(n // 2, dtype=_np.float32) * _np.float32(-2.0 * math.log(10000.0) / n))
        for n in (ROPE, HD)]).astype(_np.float32)
    arrays, args = {}, []
    for name in _NAMES:
        a = freqs if name == 'freqs' else _np.asarray(inputs[name])
        if name not in ('freqs', 'g_final'):
            a = a[0]
        a = _np.ascontiguousarray(a)
        arrays[f"in_{name}_dram"] = a
        args.append(nc.dram_tensor(f"in_{name}_dram", a.shape, _mybir.dt.from_np(a.dtype), kind="ExternalInput").ap())
    args.append(nc.dram_tensor("out_dram", (SEQ, D), F32, kind="ExternalOutput").ap())
    decoder_layer(nc, *args)
    r = _run(nc, [arrays], core_ids=[0])
    return r.results[0]["out_dram"].reshape(1, SEQ, D)
```
